# Optimizing a Trainium2 kernel written in Bass

```python
import math
import jax, jax.numpy as jnp
from jax import lax
import numpy as np

D_MODEL = 1024
BATCH = 1
SEQ = 256
DEPTH = 2
DEC_BATCH = 8
DEC_SEQ = 16
PAST_LEN = 512

CHUNK = 64
N_A_LAYERS = DEPTH // 2
N_B_LAYERS = DEPTH - N_A_LAYERS
D_FF = 2816
SSM_GROUP = 16
N_GROUPS = D_MODEL // SSM_GROUP
SSM_STATE = 64
DT_MIN = 1e-3
DT_MAX = 1e-1
N_HEADS = 16
HEAD_DIM = D_MODEL // N_HEADS
N_LEFT_CHUNKS = 8
BAND_PAST = N_LEFT_CHUNKS * CHUNK
BAND = (N_LEFT_CHUNKS + 1) * CHUNK
MAX_REL = 128
N_REL = 2 * MAX_REL + 1
EPS = 1e-6
SCALE = HEAD_DIM ** -0.5
NEG_INF = -1e30

kernel_name = 'yoco_s5_chunkband_relbias_encoder_step'

def _rmsnorm(x, g):
    xf = x.astype(jnp.float32)
    y = xf * lax.rsqrt(jnp.mean(xf * xf, axis=-1, keepdims=True) + EPS)
    return (y * g.astype(jnp.float32)).astype(x.dtype)

def _swiglu(x, w_in, w_out):
    gate, up = jnp.split(x @ w_in, 2, axis=-1)
    return (jax.nn.silu(gate) * up) @ w_out

def _half_ffn(x, g_pre, g_post, w_in, w_out):
    return x + 0.5 * _rmsnorm(_swiglu(_rmsnorm(x, g_pre), w_in, w_out), g_post)

def _ssm_combine(e1, e2):
    a1, b1 = e1
    a2, b2 = e2
    return a1 * a2, a2 * b1 + b2

def _s5_mixer(u, h0_re, h0_im, lam_re, lam_im, log_step, b_re, b_im, c_re, c_im, d_skip, w_glu):
    f32 = jnp.float32
    n, l, _ = u.shape
    uf = u.astype(f32).reshape(n, l, N_GROUPS, SSM_GROUP)
    lam = lax.complex(lam_re.astype(f32), lam_im.astype(f32))
    step = jnp.exp(log_step.astype(f32))[:, None]
    a_bar = jnp.exp(lam * step)
    b_bar = ((a_bar - 1) / lam)[..., None] * lax.complex(b_re.astype(f32), b_im.astype(f32))
    bu = jnp.einsum('gpc,nlgc->nlgp', b_bar, uf.astype(jnp.complex64))
    h0 = lax.complex(h0_re.astype(f32), h0_im.astype(f32))
    bu = bu.at[:, 0].add(a_bar * h0)
    _, h = lax.associative_scan(_ssm_combine, (jnp.broadcast_to(a_bar, bu.shape), bu), axis=1)
    c = lax.complex(c_re.astype(f32), c_im.astype(f32))
    y = jnp.einsum('gcp,nlgp->nlgc', c, h).real + d_skip.astype(f32).reshape(N_GROUPS, SSM_GROUP) * uf
    y = jax.nn.gelu(y.reshape(n, l, D_MODEL))
    val, gate = jnp.split(y @ w_glu.astype(f32), 2, axis=-1)
    out = (val * jax.nn.sigmoid(gate)).astype(u.dtype)
    h_last = h[:, -1]
    return out, h_last.real.astype(h0_re.dtype), h_last.imag.astype(h0_im.dtype)

def _band_attention_prompt(xn, k, v, w_q, w_o, table):
    f32 = jnp.float32
    n, l, _ = xn.shape
    nc = l // CHUNK
    q = (xn @ w_q).astype(f32).reshape(n, nc, CHUNK, N_HEADS, HEAD_DIM)
    pad = ((0, 0), (BAND_PAST, 0), (0, 0), (0, 0))
    kp = jnp.pad(k, pad).reshape(n, nc + N_LEFT_CHUNKS, CHUNK, N_HEADS, HEAD_DIM)
    vp = jnp.pad(v, pad).reshape(n, nc + N_LEFT_CHUNKS, CHUNK, N_HEADS, HEAD_DIM)
    kb = jnp.concatenate([kp[:, o:o + nc] for o in range(N_LEFT_CHUNKS + 1)], axis=2)
    vb = jnp.concatenate([vp[:, o:o + nc] for o in range(N_LEFT_CHUNKS + 1)], axis=2)
    qi = jnp.arange(CHUNK)
    kj = jnp.arange(BAND)
    rel = jnp.clip(qi[:, None] + BAND_PAST - kj[None, :], -MAX_REL, MAX_REL) + MAX_REL
    bias = table.astype(f32)[:, rel]
    valid = (jnp.arange(nc)[:, None] - N_LEFT_CHUNKS + kj[None, :] // CHUNK) >= 0
    s = jnp.einsum('ncihd,ncjhd->nhcij', q, kb.astype(f32)) * SCALE + bias[:, None]
    s = jnp.where(valid[:, None, :], s, NEG_INF)
    p = jax.nn.softmax(s, axis=-1).astype(v.dtype)
    o = jnp.einsum('nhcij,ncjhd->ncihd', p, vb).reshape(n, l, D_MODEL)
    return o @ w_o

def _band_attention_sample(xn, k, v, q_pos, k_pos, w_q, w_o, table):
    f32 = jnp.float32
    n, s_len, _ = xn.shape
    q = (xn @ w_q).astype(f32).reshape(n, s_len, N_HEADS, HEAD_DIM)
    rel = jnp.clip(q_pos[:, None] - k_pos[None, :], -MAX_REL, MAX_REL) + MAX_REL
    bias = table.astype(f32)[:, rel]
    qc = q_pos // CHUNK
    kc = k_pos // CHUNK
    valid = (kc[None, :] <= qc[:, None]) & (kc[None, :] >= qc[:, None] - N_LEFT_CHUNKS)
    sc = jnp.einsum('nqhd,nkhd->nhqk', q, k.astype(f32)) * SCALE + bias
    sc = jnp.where(valid, sc, NEG_INF)
    p = jax.nn.softmax(sc, axis=-1).astype(v.dtype)
    o = jnp.einsum('nhqk,nkhd->nqhd', p, v).reshape(n, s_len, D_MODEL)
    return o @ w_o

def setup_inputs(seed: int = 0) -> dict:
    key = jax.random.key(seed)
    ks = jax.random.split(key, 24)
    f32 = jnp.float32
    D = D_MODEL

    def nrm(k, shape, scale):
        return scale * jax.random.normal(k, shape, f32)

    cache_rows = min(BAND_PAST, PAST_LEN)
    ssm_state_shape = (N_A_LAYERS, DEC_BATCH, N_GROUPS, SSM_STATE)
    return {
        'x_prompt': nrm(ks[0], (BATCH, SEQ, D), 1.0),
        'x_sample': nrm(ks[1], (DEC_BATCH, DEC_SEQ, D), 1.0),
        'state_ssm_re': nrm(ks[2], ssm_state_shape, 0.1),
        'state_ssm_im': nrm(ks[3], ssm_state_shape, 0.1),
        'cache_k': nrm(ks[4], (DEC_BATCH, cache_rows, N_HEADS, HEAD_DIM), 1.0),
        'cache_v': nrm(ks[5], (DEC_BATCH, cache_rows, N_HEADS, HEAD_DIM), 1.0),
        'norm_gains': 1.0 + nrm(ks[6], (DEPTH, 6, D), 0.05),
        'ffn1_w_in': nrm(ks[7], (DEPTH, D, 2 * D_FF), D ** -0.5),
        'ffn1_w_out': nrm(ks[8], (DEPTH, D_FF, D), D_FF ** -0.5),
        'ffn2_w_in': nrm(ks[9], (DEPTH, D, 2 * D_FF), D ** -0.5),
        'ffn2_w_out': nrm(ks[10], (DEPTH, D_FF, D), D_FF ** -0.5),
        'ssm_lambda_re': -0.5 * jnp.exp(nrm(ks[11], (N_A_LAYERS, N_GROUPS, SSM_STATE), 0.01)),
        'ssm_lambda_im': math.pi * jnp.broadcast_to(jnp.arange(SSM_STATE, dtype=f32), (N_A_LAYERS, N_GROUPS, SSM_STATE)),
        'ssm_log_step': jax.random.uniform(ks[12], (N_A_LAYERS, N_GROUPS), f32, math.log(DT_MIN), math.log(DT_MAX)),
        'ssm_b_re': nrm(ks[13], (N_A_LAYERS, N_GROUPS, SSM_STATE, SSM_GROUP), (2 * SSM_GROUP) ** -0.5),
        'ssm_b_im': nrm(ks[14], (N_A_LAYERS, N_GROUPS, SSM_STATE, SSM_GROUP), (2 * SSM_GROUP) ** -0.5),
        'ssm_c_re': nrm(ks[15], (N_A_LAYERS, N_GROUPS, SSM_GROUP, SSM_STATE), SSM_STATE ** -0.5),
        'ssm_c_im': nrm(ks[16], (N_A_LAYERS, N_GROUPS, SSM_GROUP, SSM_STATE), SSM_STATE ** -0.5),
        'ssm_d': nrm(ks[17], (N_A_LAYERS, D), 1.0),
        'ssm_w_glu': nrm(ks[18], (N_A_LAYERS, D, 2 * D), D ** -0.5),
        'kv_norm': 1.0 + nrm(ks[19], (D,), 0.05),
        'w_kv': nrm(ks[20], (D, 2 * D), D ** -0.5),
        'attn_w_q': nrm(ks[21], (N_B_LAYERS, D, D), D ** -0.5),
        'attn_w_o': nrm(ks[22], (N_B_LAYERS, D, D), D ** -0.5),
        'attn_rel_bias': nrm(ks[23], (N_B_LAYERS, N_HEADS, N_REL), 0.2),
    }

def reference(x_prompt, x_sample, state_ssm_re, state_ssm_im, cache_k, cache_v,
              norm_gains, ffn1_w_in, ffn1_w_out, ffn2_w_in, ffn2_w_out,
              ssm_lambda_re, ssm_lambda_im, ssm_log_step, ssm_b_re, ssm_b_im,
              ssm_c_re, ssm_c_im, ssm_d, ssm_w_glu,
              kv_norm, w_kv, attn_w_q, attn_w_o, attn_rel_bias):

    def trunk(x, h0_re, h0_im, past_k, past_v):
        n, l, _ = x.shape
        ssm_re, ssm_im = [], []
        k = v = None
        if past_k is not None:
            r = past_k.shape[1]
            q_pos = PAST_LEN + jnp.arange(l)
            k_pos = jnp.concatenate([PAST_LEN - r + jnp.arange(r), q_pos])
        for layer in range(DEPTH):
            g = norm_gains[layer]
            x = _half_ffn(x, g[0], g[1], ffn1_w_in[layer], ffn1_w_out[layer])
            xn = _rmsnorm(x, g[2])
            if layer < N_A_LAYERS:
                y, hr, hi = _s5_mixer(xn, h0_re[layer], h0_im[layer],
                                      ssm_lambda_re[layer], ssm_lambda_im[layer], ssm_log_step[layer],
                                      ssm_b_re[layer], ssm_b_im[layer], ssm_c_re[layer], ssm_c_im[layer],
                                      ssm_d[layer], ssm_w_glu[layer])
                ssm_re.append(hr)
                ssm_im.append(hi)
            else:
                b = layer - N_A_LAYERS
                if past_k is None:
                    y = _band_attention_prompt(xn, k, v, attn_w_q[b], attn_w_o[b], attn_rel_bias[b])
                else:
                    y = _band_attention_sample(xn, jnp.concatenate([past_k, k], axis=1),
                                               jnp.concatenate([past_v, v], axis=1),
                                               q_pos, k_pos, attn_w_q[b], attn_w_o[b], attn_rel_bias[b])
            x = x + _rmsnorm(y, g[3])
            x = _half_ffn(x, g[4], g[5], ffn2_w_in[layer], ffn2_w_out[layer])
            if layer == N_A_LAYERS - 1:
                k, v = jnp.split(_rmsnorm(x, kv_norm) @ w_kv, 2, axis=-1)
                k = k.reshape(n, l, N_HEADS, HEAD_DIM)
                v = v.reshape(n, l, N_HEADS, HEAD_DIM)
        return x, jnp.stack(ssm_re), jnp.stack(ssm_im), k, v

    bp, lp, _ = x_prompt.shape
    h0_zero = jnp.zeros((N_A_LAYERS, bp, N_GROUPS, SSM_STATE), state_ssm_re.dtype)
    y_prompt, ssm_re_p, ssm_im_p, k_p, v_p = trunk(x_prompt, h0_zero, h0_zero, None, None)
    keep = min(BAND_PAST, lp)
    k_prompt = k_p[:, lp - keep:]
    v_prompt = v_p[:, lp - keep:]

    y_sample, ssm_re_s, ssm_im_s, k_sample, v_sample = trunk(x_sample, state_ssm_re, state_ssm_im, cache_k, cache_v)

    return (y_prompt, y_sample, ssm_re_p, ssm_im_p, k_prompt, v_prompt, ssm_re_s, ssm_im_s, k_sample, v_sample)


_drawn_inputs = setup_inputs


def setup_inputs(seed=0):
    import zlib

    import numpy as np

    out = dict(_drawn_inputs(seed))
    spreads = {}
    factors = {}
    for name, (base, spread) in spreads.items():
        noise = np.random.default_rng([zlib.crc32(name.encode()), seed]).standard_normal(out[name].shape)
        drawn = base * np.exp(spread * noise) if base else spread * noise
        out[name] = __import__('jax').numpy.asarray(drawn.astype(out[name].dtype))
    for name, factor in factors.items():
        out[name] = (out[name] * factor).astype(out[name].dtype)
    return out
```

```python
import math

import numpy as np

import concourse.bass as bass
from concourse import mybir

F32 = mybir.dt.float32
F32R = mybir.dt.float32r
ALU = mybir.AluOpType
ACT = mybir.ActivationFunctionType
AX_X = mybir.AxisListType.X

P = 128
D = 1024
DT = D // P
SEQ = 256
NB = 8
LS = 16
TOK = SEQ + NB * LS
TT = TOK // P
FF = 2816
FT = FF // P
NG = 64
SC = 16
NS = 64
NPAIR = NG // 2
QL = 4
NQ = TOK // QL
NC16 = TOK // LS
PRUNS = SEQ // LS
HP = NPAIR // 2
HT = DT // 2
NH = 16
HD = 64
KC = 512
KB = KC // P
KN = KC + LS
NREL = 257
PAD = 128
EPS = 1e-6
SCALE = HD ** -0.5
NEG = -1e30
TWO_PI_HI = 6.28125
TWO_PI_LO = 2 * math.pi - TWO_PI_HI
ROUND = 1.5 * 2 ** 23

STAGES = [("in", 22), ("out", 8), ("glu", 8), ("in", 22), ("out", 8), ("kv", 8),
          ("in", 22), ("out", 8), ("q", 4), ("o", 4), ("in", 22), ("out", 8)]
STARTS = [sum(c for _, c in STAGES[:i]) for i in range(len(STAGES) + 1)]
CHUNKS = STARTS[-1]
SLOT = FT * P

(PZ, PA, A4S, A16S) = (0, 8, 16, 18)
A16 = 20
LR, LI, DL, TH, MAG, SIN, ANG, COS, W0, W1, W2, W3 = range(22, 34)
NTAB = 22


def inputs_of(nc, shapes):
    return {n: nc.dram_tensor(f"in_{n}_dram", s, F32, kind="ExternalInput").ap() for n, s in shapes.items()}


class Link:

    def __init__(self, eng, sem):
        self.eng, self.sem, self.n = eng, sem, 0

    def mark(self, ins):
        self.n += 1
        ins.then_inc(self.sem, 1)
        return self.n

    def settle(self, n=None):
        self.eng.wait_ge(self.sem, self.n if n is None else n)

    def __call__(self, ins):
        self.mark(ins)
        self.settle()


def build(nc, A, O, scratch):
    base = 16512
    place = {"at": base}

    def sb(name, shape, dt=F32, at=None):
        size = 4 * int(np.prod(shape[1:]))
        if at is None:
            at = place["at"]
            place["at"] += (size + 31) // 32 * 32
        return nc.alloc_sbuf_tensor_at(name, shape, dt, offset=at)

    x = sb("x", [P, DT, TOK])
    y = sb("y", [P, DT, TOK])
    w_raw = [sb(f"w_raw{s}", [P, SLOT]) for s in range(2)]
    w_hi = [sb(f"w_hi{s}", [P, SLOT], F32R) for s in range(2)]
    w_lo = [sb(f"w_lo{s}", [P, SLOT], F32R) for s in range(2)]
    ident = sb("ident", [P, P])
    ones = sb("ones", [P, P])
    blockmask = sb("blockmask", [P, P])
    parmask = sb("parmask", [P, 2])
    consts = sb("consts", [P, 3])
    gains = sb("gains", [P, 112])
    half_gains = sb("half_gains", [P, 96])
    ssum = sb("ssum", [P, TOK])
    sq = sb("sq", [P, 2, TOK])
    std = sb("std", [P, TOK])
    rstd = sb("rstd", [P, TOK])
    scaled = sb("scaled", [P, 2, TOK])
    ffn_temps = place["at"]
    gate_s = sb("gate_s", [P, TOK])
    up_s = sb("up_s", [P, TOK])
    act_s = sb("act_s", [P, TOK])
    h_full = sb("h_full", [P, TOK])
    tab = sb("tab", [P, NTAB, NPAIR])
    R = place["at"]
    x_hi = sb("x_hi", [P, DT, TOK], F32R)
    x_lo = sb("x_lo", [P, DT, TOK], F32R)
    h_hi = sb("h_hi", [P, FT, TOK], F32R)
    h_lo = sb("h_lo", [P, FT, TOK], F32R)
    assert place["at"] <= 229344

    def region(plan, skip=0):
        at = R + 4 * skip
        out = []
        for name, shape, dt in plan:
            out.append(sb(name, shape, dt, at=at))
            at += (4 * int(np.prod(shape[1:])) + 31) // 32 * 32
        assert at <= 229344, (at, name)
        return out

    gain_rows, prow, lstep, table_rev = region([
        ("gain_rows", [112, P], F32), ("prow", [NPAIR, NTAB + 12, P], F32), ("lstep", [NPAIR, 4], F32),
        ("table_rev", [NH, PAD + NREL], F32)], skip=2 * DT * TOK)
    (ssm_t, ssm_m, ssm_ca, ssm_f, ssm_tmp, ssm_e0, ssm_u, b_nat, c_nat, c_z, c_masked, ca_tmp, st_rows, st_in,
     ) = region([
         ("ssm_t", [P, QL, 2, HT * P], F32),
         ("ssm_m", [P, QL, HT, P], F32),
         ("ssm_ca", [P, QL, 2, HP * 32], F32),
         ("ssm_f", [P, 2, HP, NQ], F32),
         ("ssm_tmp", [P, 2, HP * 32 * 2], F32),
         ("ssm_e0", [P, 2, HP, NC16], F32),
         ("ssm_u", [P, DT, TOK], F32),
         ("b_nat", [P, 2, NPAIR, SC], F32),
         ("c_nat", [P, 2, DT, NS], F32),
         ("c_z", [P, 2, HP * 32], F32),
         ("c_masked", [P, 2, 2, NS], F32),
         ("ca_tmp", [P, 2, HP * 32], F32),
         ("st_rows", [P, 2, 2, P], F32),
         ("st_in", [P, 2, NB, NPAIR], F32)])
    st_out = sb("st_out", [P, 2, NB, NPAIR], at=ffn_temps)
    st_prompt = sb("st_prompt", [P, 2, NPAIR], at=ffn_temps + 4 * 2 * NB * NPAIR)
    ssm_g = y
    gv = y[:].rearrange("p a b -> p (a b)").rearrange("p (r j s q) -> p r j s q", r=2, j=HP, s=NC16)
    kvT = sb("kvT", [P, 2 * DT, TOK], at=R + 2 * 4 * DT * TOK)
    kv_tok = sb("kv_tok", [P, TT, 2 * D], at=R + 2 * 4 * DT * TOK + 4 * 2 * DT * TOK)
    qT = y
    (k_raw, prob, probT, oT, v_raw, kT, q_blk, bias_s, row_s) = region([
        ("k_raw", [P, KB, D], F32), ("prob", [P, 2, KN], F32), ("probT", [P, 2, (KB + 1) * P], F32),
        ("oT", [P, DT, TOK], F32), ("v_raw", [P, KB + 1, D], F32), ("kT", [P, DT, KN], F32),
        ("q_blk", [P, DT, 2, LS], F32), ("bias_s", [P, 2, KN], F32), ("row_s", [P, 2, 4], F32)])
    at = R
    kTp = sb("kTp", [P, 2, SEQ], at=at)
    v_p = sb("v_p", [P, 2, 2, P], at=at + 2048)
    bias_p = sb("bias_p", [P, 2, 2, SEQ], at=at + 4096)
    prob_p = sb("prob_p", [P, 2, 3 * P], at=at + 10240)
    probT_p = sb("probT_p", [P, 2, 3 * P], at=at + 13312)
    row_p = sb("row_p", [P, 2, 8], at=at + 16384)
    q_p = sb("q_p", [P, 2, SEQ], at=at + 16512)
    x_out = sb("x_out", [P, TT, D], at=R)

    psum = nc.alloc_psum_tensor("psum", [P, 8, 512], F32)
    TOT = 4

    def acc(s, h):
        return psum[:, s + 2 * h, 0:TOK]

    names = """const_landed io_landed const_made gain_rows_t tables_t gains_ready
        w_hi_ready w_lo_ready chunk_done acc_read
        x_transposed x_new x_hi_ready x_lo_ready squared sq_added total_ready std_ready rstd_ready
        exp_in sin_in scaled_ready gate_scaled silu_ready h_full_ready h_ready sig_ready kv_done kv_tr kv_copied_v kv_copied_a stored
        ssm_landed rows_made rows_raw tab_tr u_scaled u_ready cz_masked cz_tr cz_ready zn_ready z_tr z_copied m_mm m_ready ca_ready
        f_mm f_copied st_tr st_copied g_ready y_mm y_gelu st_tr2 sout_ready
        trp_made trp_stored bias_landed bias_ready att_free k_used v_used v_landed kn_landed kt_tr kt_copied_v kt_copied_a q_ready pt4_copied soft_made recip_made qp_ready psoft_made precip_made bias_masked
        scored soft_in exped prob_ready p_tr pt_copied pv_done o_ready
        pp_free bp_used pscored psoft pexped pprob pp_tr ppt_copied ppv po_ready att_done
        out_tr out_copied_v out_copied_a dve_link act_link pool_link pe_link""".split()
    S = {n: nc.alloc_semaphore(n) for n in names}
    w_landed = [nc.alloc_semaphore(f"w_landed{s}") for s in range(2)]
    k_landed = [nc.alloc_semaphore(f"k_landed{s}") for s in range(KB)]
    p_landed = [nc.alloc_semaphore(f"p_landed{s}") for s in range(2)]

    def weight_source(stage, i):
        kind = STAGES[stage][0]
        if kind == "in":
            w = {0: A["ffn1_w_in"][0], 3: A["ffn2_w_in"][0], 6: A["ffn1_w_in"][1], 10: A["ffn2_w_in"][1]}[stage]
        elif kind == "out":
            w = {1: A["ffn1_w_out"][0], 4: A["ffn2_w_out"][0], 7: A["ffn1_w_out"][1], 11: A["ffn2_w_out"][1]}[stage]
        else:
            w = {"glu": A["ssm_w_glu"], "q": A["attn_w_q"], "o": A["attn_w_o"]}[kind][0] if kind != "kv" else A["w_kv"]
        if kind in ("in", "glu"):
            v = w.rearrange("(k p) (h n) -> h p k n", p=P, h=2)
            return [v[h][:, :, bass.ts(i, P)] for h in range(2)]
        v = w.rearrange("(k p) n -> p k n", p=P)
        if kind == "out":
            return [v[:, h * (FT // 2):(h + 1) * (FT // 2), bass.ts(i, P)] for h in range(2)]
        return [v[:, h * (DT // 2):(h + 1) * (DT // 2), bass.ts(i, 2 * P)] for h in range(2)]

    def weight_slot(t, kind):
        if kind == "out":
            v = t[:, 0:FT * P].rearrange("p (k c) -> p k c", c=P)
            return [v[:, h * (FT // 2):(h + 1) * (FT // 2)] for h in range(2)]
        v = t[:, 0:DT * 2 * P].rearrange("p (k n) -> p k n", n=2 * P)
        if kind in ("in", "glu"):
            return [v[:, :, h * P:(h + 1) * P] for h in range(2)]
        return [v[:, h * (DT // 2):(h + 1) * (DT // 2)] for h in range(2)]

    def slot_size(kind):
        return FT * P if kind == "out" else DT * 2 * P

    def gain(col):
        return gains[:, col:col + 1]

    def gain_col(layer, n, m):
        return (layer * 6 + n) * DT + m

    SPLITS = [gain_col(0, 0, 0), gain_col(0, 4, 0), 96, gain_col(1, 0, 0), gain_col(1, 2, 0), gain_col(1, 4, 0)]
    ORDER = ["ffn1", "glu", "ffn2", "kv", "ffn1b", "q", "o", "ffn2b"]
    split_base = {n: DT * i for i, n in enumerate(ORDER)}
    NORMS = 12

    def kv_dst(g):
        return kv_tok[:, g // 4, (g % 4) * 512:(g % 4 + 1) * 512]

    def out_dst(g):
        return x_out[:, g // 2, (g % 2) * 512:(g % 2 + 1) * 512]

    with nc.Block() as block:

        @block.sync
        def _(sp):
            def load(dst, src, sem):
                sp.dma_start(dst, src).then_inc(sem, 16)

            load(ident[:], A["c_ident"], S["const_landed"])
            load(blockmask[:], A["c_blockmask"], S["const_landed"])
            load(parmask[:], A["c_parmask"], S["const_landed"])
            yv = y[:].rearrange("p a b -> p (a b)").rearrange("p (t d) -> p t d", t=TT)
            load(yv[:, 0:2, :], A["x_prompt"][0].rearrange("(t p) d -> p t d", p=P), S["io_landed"])
            load(yv[:, 2, :], A["x_sample"].rearrange("b l d -> (b l) d"), S["io_landed"])
            load(gain_rows[0:96, :], A["norm_gains"].rearrange("l n (t c) -> (l n t) c", c=P), S["const_landed"])
            load(gain_rows[96:104, :], A["kv_norm"].rearrange("(t c) -> t c", c=P), S["const_landed"])
            load(gain_rows[104:112, :], A["ssm_d"][0].rearrange("(t c) -> t c", c=P), S["const_landed"])
            load(prow[:, LR, :], A["ssm_lambda_re"][0].rearrange("(j g) s -> j (g s)", g=2), S["rows_raw"])
            load(prow[:, LI, :], A["ssm_lambda_im"][0].rearrange("(j g) s -> j (g s)", g=2), S["rows_raw"])
            load(lstep[:, 0:2], A["ssm_log_step"][0].rearrange("(j g) -> j g", g=2), S["rows_raw"])
            load(table_rev[:, PAD:], A["bias_reversed"], S["rows_raw"])

            def weights(stage, first=0, last=None):
                kind, count = STAGES[stage]
                last = count if last is None else last

                def one(i, s, n, wait):
                    if wait:
                        sp.wait_ge(S["w_lo_ready"], n - 1)
                    for dst, src in zip(weight_slot(w_raw[s], kind), weight_source(stage, i)):
                        sp.dma_start(dst, src).then_inc(w_landed[s], 16)

                n0 = STARTS[stage]
                if n0 + first < 2:
                    for i in range(2):
                        one(i, i, n0 + i, False)
                    first = 2
                if first < last:
                    with sp.Fori(first // 2, last // 2) as turn:
                        i = turn * 2
                        for s in range(2):
                            one(i + s, s, i + (n0 + s), True)

            weights(0, 0, 2)
            sp.wait_ge(S["trp_made"], 1)
            sp.dma_start(scratch["bias"], table_rev[:]).then_inc(S["trp_stored"], 16)
            sp.wait_ge(S["trp_stored"], 16)
            skew = bass.AP(tensor=scratch["bias"].tensor, offset=PAD, ap=[[PAD + NREL, NH], [-1, P], [1, SEQ]])
            sp.dma_start(scratch["tiles"], skew).then_inc(S["trp_stored"], 16)
            weights(0, 2)
            weights(1)
            weights(2, 0, 4)
            sp.wait_ge(S["chunk_done"], STARTS[2])
            load(b_nat[:, 0], A["ssm_b_re"][0].rearrange("(j g) s c -> (g s) j c", g=2), S["ssm_landed"])
            load(b_nat[:, 1], A["ssm_b_im"][0].rearrange("(j g) s c -> (g s) j c", g=2), S["ssm_landed"])
            load(c_nat[:, 0], A["ssm_c_re"][0].rearrange("(t g) c s -> (g c) t s", g=8), S["ssm_landed"])
            load(c_nat[:, 1], A["ssm_c_im"][0].rearrange("(t g) c s -> (g c) t s", g=8), S["ssm_landed"])
            for ri, n in enumerate(("state_ssm_re", "state_ssm_im")):
                load(st_rows[:, ri], A[n][0].rearrange("(t b) (j g) s -> (b j) t (g s)", t=2, g=2), S["ssm_landed"])
            sp.wait_ge(S["sout_ready"], 1)
            for ri, n in enumerate(("ssm_re_s", "ssm_im_s")):
                sp.dma_start(O[n][0].rearrange("(t b) (j g) s -> (b j) t (g s)", t=2, g=2), st_rows[:, ri]).then_inc(S["stored"], 16)
            for ri, n in enumerate(("ssm_re_p", "ssm_im_p")):
                sp.dma_start(O[n][0, 0].rearrange("(j g) s -> j (g s)", g=2), c_masked[0:NPAIR, ri]).then_inc(S["stored"], 16)
            weights(2, 4)
            weights(3)
            weights(4)
            weights(5)
            weights(6, 0, 4)
            sp.wait_ge(S["kv_copied_v"], DT * TT // 4)
            sp.wait_ge(S["kv_copied_a"], DT * TT // 4)
            kvo = [kv_tok[:, :, w * D:(w + 1) * D] for w in range(2)]
            for w, (np_, ns_) in enumerate((("k_p", "k_s"), ("v_p", "v_s"))):
                sp.dma_start(O[np_][0].rearrange("(t p) h d -> p t (h d)", p=P), kvo[w][:, 0:2]).then_inc(S["stored"], 16)
                sp.dma_start(O[ns_].rearrange("b l h d -> (b l) (h d)"), kvo[w][:, 2]).then_inc(S["stored"], 16)
            sp.dma_start(scratch["v"].rearrange("(t p) d -> p t d", p=P), kvo[1]).then_inc(S["stored"], 16)
            sp.dma_start(scratch["kT"].rearrange("p (m t) -> p m t", m=DT), kvT[:, 0:DT, :]).then_inc(S["stored"], 16)
            weights(6, 4)
            weights(7)
            weights(8)
            weights(9)
            sp.wait_ge(S["stored"], 16 * 10)
            sp.wait_ge(S["trp_stored"], 32)
            sp.wait_ge(S["chunk_done"], STARTS[9])
            tb = scratch["tiles"]
            for h in range(NH):
                load(bias_s[(h % 8) * LS:(h % 8 + 1) * LS, h // 8, 384:KN], tb[h, 0:LS, 0:KN - 384], S["bias_landed"])
            ks = A["cache_k"].rearrange("b (t p) h d -> (b t) p (h d)", p=P)
            vs = A["cache_v"].rearrange("b (t p) h d -> b p t (h d)", p=P)
            kTs = scratch["kT"].rearrange("p (m t) -> p m t", m=DT)

            def stream_loads(b):
                for kb in range(KB):
                    if not isinstance(b, int):
                        sp.wait_ge(S["kt_tr"], b * 8 + (2 * kb - 6))
                    sp.dma_start(k_raw[:, kb, :], ks[bass.ds(b * KB + kb, 1)].rearrange("o p d -> (o p) d")).then_inc(k_landed[kb], 16)
                if not isinstance(b, int):
                    sp.wait_ge(S["pv_done"], b * 2)
                sp.dma_start(kT[:, :, KC:KN], kTs[:, :, bass.ds(b * LS + SEQ, LS)]).then_inc(S["kn_landed"], 16)
                sp.dma_start(v_raw[:, 0:KB, :], vs[bass.ds(b, 1)].rearrange("o p t d -> (o p) t d")).then_inc(S["v_landed"], 16)
                sp.dma_start(v_raw[0:LS, KB, :], scratch["v"][bass.ds(b * LS + SEQ, LS), :]).then_inc(S["v_landed"], 16)

            stream_loads(0)
            with sp.Fori(1, NB) as b:
                stream_loads(b)
            sp.wait_ge(S["o_ready"], 2 * NB + 1)
            kp = scratch["kT"].rearrange("p (m t) -> m p t", m=DT)
            vp = scratch["v"][0:SEQ, :].rearrange("(t p) (m n) -> m p t n", p=P, n=P)

            def prompt_loads(j, s):
                load(kTp[:, s, :], kp[bass.ds(j, 1)].rearrange("o p t -> (o p) t")[:, 0:SEQ], p_landed[s])
                load(v_p[:, s], vp[bass.ds(j, 1)].rearrange("o p t n -> (o p) t n"), p_landed[s])
                load(bias_p[:, s], tb[bass.ds(j * 2, 2)].rearrange("h r k -> r h k"), p_landed[s])

            for s in range(2):
                prompt_loads(s, s)
            with sp.Fori(1, DT // 2) as turn:
                j = turn * 2
                for s in range(2):
                    sp.wait_ge(S["po_ready"], (j + (s - 1)) * 2)
                    prompt_loads(j + s, s)
            weights(10)
            weights(11)
            ov = x_out[:]
            sp.wait_ge(S["out_copied_v"], TT)
            sp.wait_ge(S["out_copied_a"], TT)
            sp.dma_start(O["y_prompt"][0].rearrange("(t p) d -> p t d", p=P), ov[:, 0:2]).then_inc(S["stored"], 16)
            sp.dma_start(O["y_sample"].rearrange("b l d -> (b l) d"), ov[:, 2]).then_inc(S["stored"], 16)
            sp.wait_ge(S["stored"], 16 * 12)

        @block.scalar
        def _(act):
            link = Link(act, S["act_link"])

            def split_hi(s, n, kind, wait_used):
                act.wait_ge(w_landed[s], ((n - s) * 16) + 32)
                if wait_used:
                    act.wait_ge(S["chunk_done"], n - 1)
                z = slot_size(kind)
                act.activation(w_hi[s][:, 0:z], w_raw[s][:, 0:z], ACT.Copy).then_inc(S["w_hi_ready"], 1)

            def prepare_next(stage, i, s):
                kind, count = STAGES[stage]
                split_hi(s, i + (STARTS[stage] + 2), kind, True)

            def steps(stage, evacuate):
                kind, count = STAGES[stage]
                n0 = STARTS[stage]
                if count > 2:
                    with act.Fori(0, (count - 2) // 2) as turn:
                        i = turn * 2
                        for s in range(2):
                            evacuate(i + s, s, i + (n0 + s))
                            split_hi(s, i + (n0 + s + 2), kind, True)
                for s in range(2):
                    evacuate(count - 2 + s, s, n0 + count - 2 + s)
                    if stage + 1 < len(STAGES):
                        split_hi(s, n0 + count + s, STAGES[stage + 1][0], True)

            def square(src, n, s):
                if not isinstance(n, int) or n >= 2:
                    act.wait_ge(S["sq_added"], n - 1)
                act.activation(sq[:, s, :], src, ACT.Square).then_inc(S["squared"], 1)

            def root(j):
                act.wait_ge(S["total_ready"], j + 1)
                if j:
                    act.wait_ge(S["rstd_ready"], j)
                act.activation(std[:], psum[:, TOT, 0:TOK], ACT.Sqrt, bias=consts[:, 0:1], scale=1.0 / D).then_inc(S["std_ready"], 1)

            def split_x(name, col, xn0, norm):
                for m in range(DT):
                    act.wait_ge(S["x_new"], xn0 + m + 1)
                    act.activation(x_hi[:, m, :], x[:, m, :], ACT.Copy, scale=gain(col + m)).then_inc(S["x_hi_ready"], 1)
                    if norm is not None:
                        square(x[:, m, :], norm * DT + m, m % 2)

            def silu_step(t):
                def f(i, s, n):
                    act.wait_ge(S["gate_scaled"], i + (t * FT + 1))
                    act.activation(act_s[:], gate_s[:], ACT.Silu).then_inc(S["silu_ready"], 1)
                return f

            def out_step(norm):
                def f(m, s, n):
                    act.wait_ge(S["acc_read"], n + 1)
                    square(y[:, bass.ds(m, 1), :] if not isinstance(m, int) else y[:, m:m + 1, :], m + norm * DT, s)
                return f

            def glu_step(norm):
                def f(m, s, n):
                    act.wait_ge(S["chunk_done"], n + 1)
                    act.activation(act_s[:], acc(s, 1), ACT.Sigmoid).then_inc(S["sig_ready"], 1)
                    out_step(norm)(m, s, n)
                return f

            def o_step(norm):
                def f(i, s, n):
                    act.wait_ge(S["acc_read"], n + 1)
                    for h in range(2):
                        square(y[:, bass.ds(i * 2 + h, 1), :] if not isinstance(i, int) else y[:, 2 * i + h:2 * i + h + 1, :],
                               i * 2 + (norm * DT + h), h)
                return f

            def nothing(i, s, n):
                pass

            row = [prow[:, i, :] for i in range(NTAB + 12)]
            act.wait_ge(S["rows_raw"], 64)
            act.activation(lstep[:, 2:4], lstep[:, 0:2], ACT.Exp).then_inc(S["rows_made"], 1)
            act.wait_ge(S["exp_in"], 1)
            act.activation(row[MAG], row[DL], ACT.Exp).then_inc(S["rows_made"], 1)
            act.wait_ge(S["sin_in"], 1)
            act.activation(row[SIN], row[TH], ACT.Sin).then_inc(S["rows_made"], 1)
            link(act.activation(row[ANG], row[TH], ACT.Abs))
            act.wait_ge(S["const_made"], 3)
            act.activation(row[COS], row[ANG], ACT.Sin, bias=consts[0:NPAIR, 1:2], scale=-1.0).then_inc(S["rows_made"], 1)
            for s in range(2):
                split_hi(s, s, "in", False)
            act.wait_ge(S["gains_ready"], 1)
            split_x("ffn1", SPLITS[0], 0, 0)
            root(0)
            steps(0, silu_step(0))
            steps(1, out_step(1))
            root(1)
            for m in range(DT):
                act.wait_ge(S["x_new"], DT + m + 1)
                square(x[:, m, :], 2 * DT + m, m % 2)
            root(2)
            for m in range(DT):
                act.wait_ge(S["u_scaled"], m + 1)
                act.activation(ssm_u[:, m, :], scaled[:, m % 2, :], ACT.Copy, scale=gain(gain_col(0, 2, m))).then_inc(S["u_ready"], 1)
            act.wait_ge(S["st_tr"], 1)
            act.activation(st_in[:].rearrange("p r b j -> p (r b j)"), psum[:, 7, :], ACT.Copy).then_inc(S["st_copied"], 1)
            for half in range(2):
                for ri in range(2):
                    act.wait_ge(S["cz_tr"], 2 * half + ri + 1)
                    if half:
                        act.wait_ge(S["ca_ready"], half)
                        act.wait_ge(S["m_mm"], half * QL)
                    act.activation(c_z[:, ri, :], psum[:, 5 + ri, :], ACT.Copy, scale=(1.0, -1.0)[ri]).then_inc(S["cz_ready"], 1)
                for s in range(QL):
                    for ri in range(2):
                        act.wait_ge(S["z_tr"], (half * QL + s) * 2 + ri + 1)
                        if half:
                            act.wait_ge(S["f_mm"], 2)
                        act.activation(ssm_t[:, s, ri, :], psum[:, 5 + ri, :], ACT.Copy).then_inc(S["z_copied"], 1)
                for t2 in range(HT // 2):
                    act.wait_ge(S["f_mm"], half * 2 + t2 + 1)
                    fv = ssm_f[:].rearrange("p r (t j) n -> p t r j n", j=4)
                    for j in range(4):
                        for ri in range(2):
                            src = psum[:, j, 0:4 * NQ].rearrange("p (t r n) -> p r t n", t=2, r=2)[:, ri]
                            act.activation(fv[:, 2 * t2:2 * t2 + 2, ri, j, :], src, ACT.Copy).then_inc(S["f_copied"], 1)
                for t in range(HT):
                    m = half * HT + t
                    act.wait_ge(S["y_mm"], m + 1)
                    act.activation(ssm_u[:, m, :].rearrange("p (n r) -> p n r", r=QL),
                                   psum[:, 5 + t % 2, 0:TOK].rearrange("p (r n) -> p n r", r=QL), ACT.Gelu_apprx_tanh).then_inc(S["y_gelu"], 1)
            act.wait_ge(S["st_tr2"], 1)
            link(act.activation(st_rows[:].rearrange("p r t n -> p (r t n)"), psum[:, 7, :], ACT.Copy))
            act.activation(c_masked[0:NPAIR].rearrange("p r g n -> p (r g n)"), psum[0:NPAIR, 4, 0:2 * P], ACT.Copy).then_inc(S["sout_ready"], 1)
            for m in range(DT):
                act.activation(x_hi[:, m, :], ssm_u[:, m, :], ACT.Copy).then_inc(S["x_hi_ready"], 1)
            steps(2, glu_step(3))
            root(3)
            split_x("ffn2", SPLITS[1], 2 * DT, 4)
            root(4)
            steps(3, silu_step(1))
            steps(4, out_step(5))
            root(5)
            split_x("kv", SPLITS[2], 3 * DT, 6)
            root(6)
            steps(5, nothing)
            act.wait_ge(S["chunk_done"], STARTS[6])
            for m in range(DT):
                act.activation(x_hi[:, m, :], x[:, m, :], ACT.Copy, scale=gain(SPLITS[3] + m)).then_inc(S["x_hi_ready"], 1)
            for g in range(2 * DT * TT // 4):
                if g % 2:
                    act.wait_ge(S["kv_tr"], g + 1)
                    act.activation(kv_dst(g), psum[:, 5 + g % 3, :], ACT.Copy).then_inc(S["kv_copied_a"], 1)
            steps(6, silu_step(2))
            steps(7, out_step(7))
            root(7)
            split_x("q", SPLITS[4], 4 * DT, 8)
            root(8)
            steps(8, nothing)
            with act.Fori(0, NB) as b:
                for kb in range(KB):
                    act.wait_ge(S["kt_tr"], b * 8 + (2 * kb + 2))
                    act.activation(kT[:, 4:8, kb * P:(kb + 1) * P], psum[:, 6, :].rearrange("p (a c) -> p a c", c=P), ACT.Copy).then_inc(S["kt_copied_a"], 1)
                for hh in range(2):
                    act.wait_ge(S["soft_in"], b * 2 + (hh + 1))
                    act.activation(prob[:, hh, :], prob[:, hh, :], ACT.Exp, bias=row_s[:, hh, 0:1],
                                   accum_out=row_s[:, hh, 1:2]).then_inc(S["exped"], 1)
                for hh in range(2):
                    act.wait_ge(S["p_tr"], b * 2 + (hh + 1))
                    act.activation(probT[:, hh, 0:KC], psum[:, 7, :], ACT.Copy).then_inc(S["pt_copied"], 1)
            with act.Fori(0, DT) as j:
                for hh in range(2):
                    act.wait_ge(S["psoft"], j * 2 + (hh + 1))
                    for T in range(2):
                        c0, c1 = ((0, P), (P, 3 * P))[T]
                        ins = act.activation(prob_p[:, hh, c0:c1], prob_p[:, hh, c0:c1], ACT.Exp, bias=row_p[:, hh, T:T + 1],
                                             accum_out=row_p[:, hh, 2 + T:3 + T])
                    ins.then_inc(S["pexped"], 1)
            act.wait_ge(S["po_ready"], 2 * DT)
            for m in range(DT):
                act.activation(x_hi[:, m, :], oT[:, m, :], ACT.Copy).then_inc(S["x_hi_ready"], 1)
            steps(9, o_step(9))
            root(9)
            split_x("ffn2b", SPLITS[5], 5 * DT, 10)
            root(10)
            steps(10, silu_step(3))
            steps(11, out_step(11))
            root(11)
            for g in range(2 * TT):
                if g % 2:
                    act.wait_ge(S["out_tr"], g + 1)
                    act.activation(out_dst(g), psum[:, 5 + g % 3, :], ACT.Copy).then_inc(S["out_copied_a"], 1)


        @block.vector
        def _(dve):
            link = Link(dve, S["dve_link"])
            tt, stt, ts = dve.tensor_tensor, dve.scalar_tensor_tensor, dve.tensor_scalar

            def split_lo(s, n, kind):
                z = slot_size(kind)
                dve.wait_ge(S["w_hi_ready"], n + 1)
                tt(w_lo[s][:, 0:z], w_raw[s][:, 0:z], w_hi[s][:, 0:z].bitcast(F32), ALU.subtract).then_inc(S["w_lo_ready"], 1)

            def steps(stage, evacuate):
                kind, count = STAGES[stage]
                n0 = STARTS[stage]
                if count > 2:
                    with dve.Fori(0, (count - 2) // 2) as turn:
                        i = turn * 2
                        for s in range(2):
                            evacuate(i + s, s, i + (n0 + s))
                            split_lo(s, i + (n0 + s + 2), kind)
                for s in range(2):
                    evacuate(count - 2 + s, s, n0 + count - 2 + s)
                    if stage + 1 < len(STAGES):
                        split_lo(s, n0 + count + s, STAGES[stage + 1][0])

            def tile(t, m):
                return t[:, m, :] if isinstance(m, int) else t[:, bass.ds(m, 1), :]

            def root(j):
                dve.wait_ge(S["std_ready"], j + 1)
                dve.reciprocal(rstd[:], std[:]).then_inc(S["rstd_ready"], 1)
                dve.wait_ge(S["rstd_ready"], j + 1)

            def in_step(t):
                def f(i, s, n):
                    c = t * FT + 1
                    dve.wait_ge(S["chunk_done"], n + 1)
                    tt(gate_s[:], acc(s, 0), rstd[:], ALU.mult).then_inc(S["gate_scaled"], 1)
                    tt(up_s[:], acc(s, 1), rstd[:], ALU.mult).then_inc(S["acc_read"], 1)
                    dve.wait_ge(S["acc_read"], n + 1)
                    dve.wait_ge(S["silu_ready"], i + c)
                    tt(h_full[:], act_s[:], up_s[:], ALU.mult).then_inc(S["h_full_ready"], 1)
                    tt(tile(h_hi, i), act_s[:], up_s[:], ALU.mult).then_inc(S["h_full_ready"], 1)
                    dve.wait_ge(S["h_full_ready"], i * 2 + 2 * c)
                    tt(tile(h_lo, i), h_full[:], tile(h_hi, i).bitcast(F32), ALU.subtract).then_inc(S["h_ready"], 1)
                    dve.wait_ge(S["h_ready"], i + c)
                return f

            def out_step(m, s, n):
                dve.wait_ge(S["chunk_done"], n + 1)
                dve.tensor_copy(tile(y, m), acc(s, 0)).then_inc(S["acc_read"], 1)

            def glu_step(m, s, n):
                dve.wait_ge(S["chunk_done"], n + 1)
                dve.wait_ge(S["sig_ready"], m + 1)
                tt(tile(y, m), acc(s, 0), act_s[:], ALU.mult).then_inc(S["acc_read"], 1)

            def o_step(i, s, n):
                dve.wait_ge(S["chunk_done"], n + 1)
                dve.tensor_copy(tile(y, i * 2), acc(s, 0))
                dve.tensor_copy(tile(y, i * 2 + 1), acc(s, 1)).then_inc(S["acc_read"], 1)

            def scaled_step(dst):
                def f(i, s, n):
                    dve.wait_ge(S["chunk_done"], n + 1)
                    tt(tile(dst, i * 2), acc(s, 0), rstd[:], ALU.mult)
                    tt(tile(dst, i * 2 + 1), acc(s, 1), rstd[:], ALU.mult).then_inc(S["acc_read"], 1)
                return f

            def advance(table, col, k, split=None, scol=None):
                for m in range(DT + 2):
                    if m < DT:
                        if m >= 2:
                            dve.wait_ge(S["x_new"], DT * (k + 1) + m - 1)
                        tt(scaled[:, m % 2, :], y[:, m, :], rstd[:], ALU.mult).then_inc(S["scaled_ready"], 1)
                    if 1 <= m <= DT:
                        q = m - 1
                        dve.wait_ge(S["scaled_ready"], DT * k + q + 1)
                        stt(x[:, q, :], scaled[:, q % 2, :], table[:, col + q:col + q + 1], x[:, q, :], ALU.mult,
                            ALU.add).then_inc(S["x_new"], 1)
                    if split is not None and m >= 2:
                        lo(split, scol, m - 2)

            def lo(name, scol, m):
                dve.wait_ge(S["x_hi_ready"], split_base[name] + m + 1)
                stt(x_lo[:, m, :], x[:, m, :], gain(scol + m), x_hi[:, m, :].bitcast(F32), ALU.mult,
                    ALU.subtract).then_inc(S["x_lo_ready"], 1)

            row = [prow[:, i, :] for i in range(NTAB + 12)]

            def mul(o, a, b):
                link.mark(tt(row[o], row[a], row[b], ALU.mult))

            def cmul(o, a, b):
                mul(W0, a, b)
                mul(W1, a + 1, b + 1)
                mul(W2, a, b + 1)
                mul(W3, a + 1, b)
                link.settle()
                link.mark(tt(row[o], row[W0], row[W1], ALU.subtract))
                link(tt(row[o + 1], row[W2], row[W3], ALU.add))

            dve.wait_ge(S["rows_raw"], 64)
            dve.tensor_copy(table_rev[:, 0:PAD], table_rev[:, PAD:PAD + 1].broadcast_to([NH, PAD])).then_inc(S["trp_made"], 1)
            dve.wait_ge(S["rows_made"], 1)
            step = lstep[:, 2:4].unsqueeze(2).broadcast_to([NPAIR, 2, NS])
            two = [prow[:, i, :].rearrange("p (g s) -> p g s", g=2) for i in range(NTAB + 12)]
            tt(two[DL], two[LR], step, ALU.mult).then_inc(S["exp_in"], 1)
            link(tt(two[W0], two[LI], step, ALU.mult))
            link(ts(row[W1], row[W0], 1 / (2 * math.pi), ROUND, ALU.mult, ALU.add))
            link(ts(row[W2], row[W1], ROUND, None, ALU.subtract))
            link(stt(row[W1], row[W2], -TWO_PI_HI, row[W0], ALU.mult, ALU.add))
            link(stt(row[W3], row[W2], -TWO_PI_LO, row[W1], ALU.mult, ALU.add))
            ts(row[TH], row[W3], math.pi, -math.pi, ALU.min, ALU.max).then_inc(S["sin_in"], 1)
            dve.wait_ge(S["rows_made"], 4)
            mul(PA, MAG, COS)
            mul(PA + 1, MAG, SIN)
            link.settle()
            cmul(PA + 2, PA, PA)
            cmul(PA + 4, PA + 2, PA)
            cmul(PA + 6, PA + 2, PA + 2)
            cmul(A16, PA + 6, PA + 6)
            cmul(A4S, A16, A16)
            link.mark(dve.tensor_copy(row[A16], row[A4S]))
            link.mark(dve.tensor_copy(row[A16 + 1], row[A4S + 1]))
            link.mark(ts(row[A16S], row[A4S + 1], -1.0, None, ALU.mult))
            link(dve.tensor_copy(row[A16S + 1], row[A4S + 1]))
            link.mark(ts(row[A4S], row[PA + 7], -1.0, None, ALU.mult))
            link.mark(dve.tensor_copy(row[A4S + 1], row[PA + 7]))
            mul(W0, LR, LR)
            mul(W1, LI, LI)
            link.mark(ts(row[ANG], row[PA], 1.0, None, ALU.subtract))
            link.settle()
            link(tt(row[W2], row[W0], row[W1], ALU.add))
            link(dve.reciprocal(row[DL], row[W2]))
            mul(W0, ANG, LR)
            mul(W1, PA + 1, LI)
            mul(W2, PA + 1, LR)
            mul(W3, ANG, LI)
            link.settle()
            link.mark(tt(row[W0], row[W0], row[W1], ALU.add))
            link(tt(row[W2], row[W2], row[W3], ALU.subtract))
            mul(PZ, W0, DL)
            mul(PZ + 1, W2, DL)
            link.settle()
            cmul(PZ + 2, PZ, PA)
            cmul(PZ + 4, PZ, PA + 2)
            cmul(PZ + 6, PZ, PA + 4)
            dve.tensor_copy(row[W0], row[LR]).then_inc(S["tables_t"], 1)
            for s in range(2):
                split_lo(s, s, "in")
            dve.wait_ge(S["gain_rows_t"], 1)
            dve.tensor_copy(gains[:], psum[:, 7, 0:112]).then_inc(S["gains_ready"], 1)
            dve.wait_ge(S["gains_ready"], 1)
            link(ts(half_gains[:], gains[:, 0:96], 0.5, None, ALU.mult))
            for m in range(DT + 1):
                if m < DT:
                    dve.wait_ge(S["x_transposed"], m + 1)
                    dve.tensor_copy(x[:, m, :], psum[:, m % 4, 0:TOK]).then_inc(S["x_new"], 1)
                if m >= 1:
                    lo("ffn1", SPLITS[0], m - 1)
            dve.wait_ge(S["tab_tr"], 1)
            link.mark(dve.tensor_copy(tab[:, 0:16, :].rearrange("p a j -> p (a j)"), psum[:, 5, :]))
            link(dve.tensor_copy(tab[:, 16:NTAB, :].rearrange("p a j -> p (a j)"), psum[:, 6, 0:(NTAB - 16) * NPAIR]))
            root(0)
            dve.wait_ge(S["trp_stored"], 32)
            steps(0, in_step(0))
            steps(1, out_step)
            root(1)
            advance(half_gains, gain_col(0, 1, 0), 0)
            root(2)
            dve.wait_ge(S["x_new"], 2 * DT)
            for m in range(DT):
                if m >= 2:
                    dve.wait_ge(S["u_ready"], m - 1)
                tt(scaled[:, m % 2, :], x[:, m, :], rstd[:], ALU.mult).then_inc(S["u_scaled"], 1)

            dve.wait_ge(S["ssm_landed"], 16 * 6)
            stage = ssm_f[:].rearrange("p r j n -> p (r j n)")
            zt = [stage[:, 1024 + 256 * i:1280 + 256 * i].rearrange("p (j c) -> p j c", c=SC) for i in range(4)]
            fv = ssm_f[:].rearrange("p r j (s q) -> p r j s q", q=QL)
            for half in range(2):
                j0, t0 = half * HP, half * HT
                js = slice(j0, j0 + HP)
                for ri in range(2):
                    src = c_nat[:, ri, t0:t0 + HT, :].unsqueeze(2).broadcast_to([P, HT, 2, NS])
                    msk = parmask[:].unsqueeze(1).unsqueeze(3).broadcast_to([P, HT, 2, NS])
                    dst = stage[:, 512 * ri:512 * ri + 512].rearrange("p (t g s) -> p t g s", t=HT, g=2)
                    tt(dst, src, msk, ALU.mult).then_inc(S["cz_masked"], 1)
                link(dve.memset(ssm_tmp[:], 0.0))
                for s in range(QL):
                    if s >= 2:
                        dve.wait_ge(S["m_mm"], half * QL + s - 1)
                    zn = ssm_tmp[:, s % 2, :].rearrange("p (r j g c) -> p r j g c", r=2, j=HP, g=2)
                    pr, pi = (tab[:, PZ + 2 * s + ri, js].unsqueeze(2).broadcast_to([P, HP, SC]) for ri in range(2))
                    br, bi = (b_nat[:, ri, js, :] for ri in range(2))
                    for o, (a, b) in enumerate(((pr, br), (pi, bi), (pr, bi), (pi, br))):
                        link.mark(tt(zt[o], b, a, ALU.mult))
                    link.settle()
                    for g in range(2):
                        rows = slice(g * NS, (g + 1) * NS)
                        link.mark(tt(zn[rows, 0, :, g, :], zt[0][rows], zt[1][rows], ALU.subtract))
                    for g in range(2):
                        rows = slice(g * NS, (g + 1) * NS)
                        ins = tt(zn[rows, 1, :, g, :], zt[2][rows], zt[3][rows], ALU.add)
                        if g == 0:
                            link.mark(ins)
                    ins.then_inc(S["zn_ready"], 1)
                    dve.wait_ge(S["zn_ready"], half * QL + s + 1)
                    dve.wait_ge(S["m_mm"], half * QL + s + 1)
                    if half:
                        dve.wait_ge(S["y_mm"], HT)
                    link(tt(ssm_m[:, s], psum[:, 7, :].rearrange("p (t c) -> p t c", c=P),
                            blockmask[:].unsqueeze(1).broadcast_to([P, HT, P]), ALU.mult))
                    if s == 0:
                        for t in range(HT):
                            col = 104 + t0 + t
                            link.mark(stt(ssm_m[:, 0, t], ident[:], gains[:, col:col + 1], ssm_m[:, 0, t], ALU.mult, ALU.add))
                        link.settle()
                    dve.tensor_copy(scaled[:, 0, 0:1], consts[:, 0:1]).then_inc(S["m_ready"], 1)
                    dve.wait_ge(S["m_ready"], half * QL + s + 1)

                t1, t2 = (ssm_tmp[:, i, 0:2 * HP * NC16].rearrange("p (r j s) -> p r j s", r=2, j=HP) for i in range(2))

                def advance_state(out, state, add, ar, ais, n, at=0):
                    u1, u2 = t1[:, :, :, 0:n], t2[:, :, :, 0:n]
                    a = tab[:, ar, js].unsqueeze(1).unsqueeze(3).broadcast_to([P, 2, HP, n])
                    link.mark(tt(u1, state, a, ALU.mult))
                    for ri in range(2):
                        link.mark(tt(u2[:, ri], state[:, 1 - ri],
                                     tab[:, ais + ri, js].unsqueeze(2).broadcast_to([P, HP, n]), ALU.mult))
                    link.settle()
                    link(tt(u1, u1, u2, ALU.add))
                    link(tt(out, u1, add, ALU.add))

                dve.wait_ge(S["f_copied"], 16 * (half + 1))
                e0 = ssm_e0[:]
                advance_state(e0, fv[:, :, :, :, 0], fv[:, :, :, :, 1], PA + 6, A4S, NC16)
                for q in range(2, QL):
                    advance_state(e0, e0, fv[:, :, :, :, q], PA + 6, A4S, NC16)
                if half:
                    dve.wait_ge(S["y_mm"], HT)
                dve.wait_ge(S["st_copied"], 1)
                link.mark(dve.memset(gv[:, :, :, 0, 0], 0.0))
                for ri in range(2):
                    link.mark(dve.tensor_copy(gv[:, ri, :, PRUNS:, 0], st_in[:, ri, :, js].rearrange("p b j -> p j b")))
                link(dve.tensor_copy(gv[:, :, :, 1, 0], e0[:, :, :, 0]))
                for k in range(1, PRUNS):
                    last = k == PRUNS - 1
                    advance_state(st_prompt[:, :, js].unsqueeze(3) if last else gv[:, :, :, k + 1:k + 2, 0],
                                  gv[:, :, :, k:k + 1, 0], e0[:, :, :, k:k + 1], A16, A16S, 1)
                advance_state(st_out[:, :, :, js].rearrange("p r b j -> p r j b"), gv[:, :, :, PRUNS:, 0],
                              e0[:, :, :, PRUNS:], A16, A16S, NB)
                for q in range(QL - 1):
                    advance_state(gv[:, :, :, :, q + 1], gv[:, :, :, :, q], fv[:, :, :, :, q], PA + 6, A4S, NC16)
                dve.tensor_copy(scaled[:, 0, 0:1], consts[:, 0:1]).then_inc(S["g_ready"], 1)
                dve.wait_ge(S["g_ready"], half + 1)
            for m in range(DT):
                dve.wait_ge(S["x_hi_ready"], split_base["glu"] + m + 1)
                tt(x_lo[:, m, :], ssm_u[:, m, :], x_hi[:, m, :].bitcast(F32), ALU.subtract).then_inc(S["x_lo_ready"], 1)
            steps(2, glu_step)
            root(3)
            advance(gains, gain_col(0, 3, 0), 1, "ffn2", SPLITS[1])
            root(4)
            steps(3, in_step(1))
            steps(4, out_step)
            root(5)
            advance(half_gains, gain_col(0, 5, 0), 2, "kv", SPLITS[2])
            root(6)
            steps(5, scaled_step(kvT))
            for m in range(DT):
                lo("ffn1b", SPLITS[3], m)
            for g in range(0, 2 * DT * TT // 4, 2):
                dve.wait_ge(S["kv_tr"], g + 1)
                dve.tensor_copy(kv_dst(g), psum[:, 5 + g % 3, :]).then_inc(S["kv_copied_v"], 1)
            dve.wait_ge(S["stored"], 16 * 10)
            steps(6, in_step(2))
            steps(7, out_step)
            root(7)
            advance(half_gains, gain_col(1, 1, 0), 3, "q", SPLITS[4])
            root(8)
            steps(8, scaled_step(qT))

            link(dve.memset(q_blk[:], 0.0))
            dve.tensor_copy(row_s[:, 0, 3:4], consts[:, 0:1]).then_inc(S["scored"], 1)
            dve.wait_ge(S["bias_landed"], 16 * NH)
            for hh in range(2):
                link.mark(dve.tensor_copy(bias_s[:, hh, 0:384], bias_s[:, hh, 384:385].broadcast_to([P, 384])))
            link.settle()
            dve.tensor_copy(row_s[:, 1, 3:4], consts[:, 0:1]).then_inc(S["o_ready"], 1)
            with dve.Fori(0, NB) as b:
                dve.wait_ge(S["scored"], b * 2 + 1)
                for g in range(2):
                    rows = slice(g * HD, (g + 1) * HD)
                    ins = dve.tensor_copy(q_blk[rows, :, g, :], qT[rows, :, bass.ds(b * LS + SEQ, LS)])
                ins.then_inc(S["q_ready"], 1)
                for kb in range(KB):
                    dve.wait_ge(S["kt_tr"], b * 8 + (2 * kb + 1))
                    dve.tensor_copy(kT[:, 0:4, kb * P:(kb + 1) * P], psum[:, 5, :].rearrange("p (a c) -> p a c", c=P)).then_inc(S["kt_copied_v"], 1)
                for hh in range(2):
                    dve.wait_ge(S["scored"], b * 2 + (hh + 2))
                    sc = psum[:, 2 * hh:2 * hh + 2, :].rearrange("p a b -> p (a b)")[:, 0:KN]
                    stt(prob[:, hh, :], sc, SCALE, bias_s[:, hh, :], ALU.mult, ALU.add).then_inc(S["soft_made"], 1)
                    dve.wait_ge(S["soft_made"], b * 2 + (hh + 1))
                    dve.tensor_reduce(row_s[:, hh, 0:1], prob[:, hh, :], AX_X, ALU.max, negate=True).then_inc(S["soft_in"], 1)
                for hh in range(2):
                    dve.wait_ge(S["exped"], b * 2 + (hh + 1))
                    dve.reciprocal(row_s[:, hh, 2:3], row_s[:, hh, 1:2]).then_inc(S["recip_made"], 1)
                    dve.wait_ge(S["recip_made"], b * 2 + (hh + 1))
                    ts(prob[:, hh, :], prob[:, hh, :], row_s[:, hh, 2:3], None, ALU.mult).then_inc(S["prob_ready"], 1)
                for hh in range(2):
                    dve.wait_ge(S["p_tr"], b * 2 + (hh + 1))
                    dve.tensor_copy(probT[0:LS, hh, KC:KC + P], psum[0:LS, TOT, 0:P]).then_inc(S["pt4_copied"], 1)
                for hh in range(2):
                    dve.wait_ge(S["pv_done"], b * 2 + (hh + 1))
                    for g in range(2):
                        rows = slice(g * HD, (g + 1) * HD)
                        src = psum[rows, 2 * hh + 1, P:2 * P].rearrange("p (a g i) -> p a g i", g=2, i=LS)[:, :, g, :]
                        ins = dve.tensor_copy(oT[rows, 4 * hh:4 * hh + 4, bass.ds(b * LS + SEQ, LS)], src)
                    ins.then_inc(S["o_ready"], 1)
            with dve.Fori(0, DT // 2) as turn:
                jj = turn * 2
                for s in range(2):
                    dve.tensor_copy(q_p[:, s:s + 1, :], qT[:, bass.ds(jj + s, 1), 0:SEQ]).then_inc(S["qp_ready"], 1)
                    dve.wait_ge(p_landed[s], jj * 24 + 48)
                    dve.memset(bias_p[0:HD, s, :, SEQ - HD:SEQ], NEG).then_inc(S["bias_masked"], 1)
                    dve.wait_ge(S["bias_masked"], jj + (s + 1))
                    for hh in range(2):
                        c = 2 * s + hh
                        dve.wait_ge(S["pscored"], jj * 2 + (c + 1))
                        stt(prob_p[:, hh, 0:P], psum[:, hh, 0:P], SCALE, bias_p[:, s, hh, P:2 * P], ALU.mult, ALU.add)
                        stt(prob_p[:, hh, P:3 * P], psum[:, hh, P:3 * P], SCALE, bias_p[:, s, hh, :], ALU.mult,
                            ALU.add).then_inc(S["psoft_made"], 1)
                        dve.wait_ge(S["psoft_made"], jj * 2 + (c + 1))
                        dve.tensor_reduce(row_p[:, hh, 0:1], prob_p[:, hh, 0:P], AX_X, ALU.max, negate=True)
                        dve.tensor_reduce(row_p[:, hh, 1:2], prob_p[:, hh, P:3 * P], AX_X, ALU.max, negate=True).then_inc(S["psoft"], 1)
                    for hh in range(2):
                        c = 2 * s + hh
                        dve.wait_ge(S["pexped"], jj * 2 + (c + 1))
                        dve.reciprocal(row_p[:, hh, 4:6], row_p[:, hh, 2:4]).then_inc(S["precip_made"], 1)
                        dve.wait_ge(S["precip_made"], jj * 2 + (c + 1))
                        ts(prob_p[:, hh, 0:P], prob_p[:, hh, 0:P], row_p[:, hh, 4:5], None, ALU.mult)
                        ts(prob_p[:, hh, P:3 * P], prob_p[:, hh, P:3 * P], row_p[:, hh, 5:6], None, ALU.mult).then_inc(S["pprob"], 1)
                    for hh in range(2):
                        c = 2 * s + hh
                        dve.wait_ge(S["pp_tr"], jj * 2 + (c + 1))
                        dve.tensor_copy(probT_p[:, hh, :], psum[:, 2 + hh, 0:3 * P]).then_inc(S["ppt_copied"], 1)
                    for hh in range(2):
                        c = 2 * s + hh
                        rows = slice(hh * HD, (hh + 1) * HD)
                        dve.wait_ge(S["ppv"], jj * 2 + (c + 1))
                        dve.tensor_copy(oT[rows, bass.ds(jj + s, 1), 0:SEQ], psum[rows, 5 + hh, 0:SEQ].unsqueeze(1)).then_inc(S["po_ready"], 1)
            for m in range(DT):
                dve.wait_ge(S["x_hi_ready"], split_base["o"] + m + 1)
                tt(x_lo[:, m, :], oT[:, m, :], x_hi[:, m, :].bitcast(F32), ALU.subtract).then_inc(S["x_lo_ready"], 1)
            steps(9, o_step)
            root(9)
            advance(gains, gain_col(1, 3, 0), 4, "ffn2b", SPLITS[5])
            root(10)
            steps(10, in_step(3))
            steps(11, out_step)
            root(11)
            advance(half_gains, gain_col(1, 5, 0), 5)
            for g in range(0, 2 * TT, 2):
                dve.wait_ge(S["out_tr"], g + 1)
                dve.tensor_copy(out_dst(g), psum[:, 5 + g % 3, :]).then_inc(S["out_copied_v"], 1)

        @block.gpsimd
        def _(pool):
            pool.memset(ones[:], 1.0).then_inc(S["const_made"], 1)
            pool.memset(consts[:, 0:1], EPS).then_inc(S["const_made"], 1)
            pool.memset(consts[:, 1:2], math.pi / 2).then_inc(S["const_made"], 1)
            pool.memset(consts[:, 2:3], 0.0).then_inc(S["const_made"], 1)
            pool.wait_ge(S["const_made"], 4)

            def sums(j0, j1):
                def one(j):
                    if not isinstance(j, int) or j > 0:
                        pool.wait_ge(S["total_ready"], j * 1)
                    pool.wait_ge(S["squared"], j * DT + 1)
                    pool.tensor_tensor(ssum[:], sq[:, 0, :], consts[:, 2:3].broadcast_to([P, TOK]), ALU.add).then_inc(S["sq_added"], 1)
                    for m in range(1, DT):
                        pool.wait_ge(S["squared"], j * DT + (m + 1))
                        pool.wait_ge(S["sq_added"], j * DT + m)
                        pool.tensor_tensor(ssum[:], ssum[:], sq[:, m % 2, :], ALU.add).then_inc(S["sq_added"], 1)
                if j1 == j0 + 1:
                    one(j0)
                else:
                    with pool.Fori(j0, j1) as j:
                        one(j)

            sums(0, 1)
            sums(1, 3)
            link = Link(pool, S["pool_link"])
            cr, cn = (c_z[:, ri, :].rearrange("p (j c) -> p j c", j=HP) for ri in range(2))
            a, b = (ca_tmp[:, i, :].rearrange("p (j c) -> p j c", j=HP) for i in range(2))
            for half in range(2):
                js = slice(half * HP, (half + 1) * HP)
                pool.wait_ge(S["cz_ready"], 2 * half + 2)
                if half:
                    pool.wait_ge(S["y_mm"], HT)
                for t in range(QL):
                    pr, pi = (tab[:, PA + 2 * t + ri, js].unsqueeze(2).broadcast_to([P, HP, 32]) for ri in range(2))
                    for ri, (u, v, op) in enumerate(((cr, cn, ALU.add), (cn, cr, ALU.subtract))):
                        dst = ssm_ca[:, t, ri, :].rearrange("p (j c) -> p j c", j=HP)
                        link.mark(pool.tensor_tensor(a, u, pr, ALU.mult))
                        link(pool.tensor_tensor(b, v, pi, ALU.mult))
                        link(pool.tensor_tensor(dst, a, b, op))
                pool.memset(ca_tmp[:, 0, 0:1], 0.0).then_inc(S["ca_ready"], 1)
                pool.wait_ge(S["ca_ready"], half + 1)
            sums(3, NORMS)

        @block.tensor
        def _(pe):
            link = Link(pe, S["pe_link"])
            mm, tr = pe.matmul, pe.transpose

            def chunk(stage, s, n, parts=None, gate=None):
                kind = STAGES[stage][0]
                hi, lo = (h_hi, h_lo) if kind == "out" else (x_hi, x_lo)
                K = FT if kind == "out" else DT
                pe.wait_ge(S["w_lo_ready"], n + 1)
                if not isinstance(n, int) or n >= 2:
                    pe.wait_ge(S["acc_read"], n - 1)
                for k in range(K):
                    if gate is not None:
                        pe.wait_ge(gate[0], gate[1] + k)
                    for h in range(1 if kind == "out" else 2):
                        c = k * P if kind == "out" else k * 2 * P + h * P
                        out = acc(s, h)
                        mm(out, w_hi[s][:, c:c + P], hi[:, k, :], start=(k == 0), stop=False)
                        mm(out, w_hi[s][:, c:c + P], lo[:, k, :], start=False, stop=False)
                        ins = mm(out, w_lo[s][:, c:c + P], hi[:, k, :], start=False, stop=(k == K - 1))
                ins.then_inc(S["chunk_done"], 1)

            def products(stage, gate, after_first=None):
                n0, count = STARTS[stage], STAGES[stage][1]
                chunk(stage, 0, n0, gate=gate)
                if after_first is not None:
                    total(after_first)
                chunk(stage, 1, n0 + 1)
                with pe.Fori(1, count // 2) as turn:
                    i = turn * 2
                    for s in range(2):
                        chunk(stage, s, i + (n0 + s))

            def total(j):
                pe.wait_ge(S["sq_added"], DT * (j + 1))
                if j:
                    pe.wait_ge(S["std_ready"], j)
                mm(psum[:, TOT, 0:TOK], ones[:], ssum[:], start=True, stop=True).then_inc(S["total_ready"], 1)

            def x_gate(name):
                return S["x_lo_ready"], split_base[name] + 1

            pe.wait_ge(S["const_landed"], 16 * 6)
            tr(psum[:, 7, 0:112], gain_rows[:, :], ident[0:112, 0:112]).then_inc(S["gain_rows_t"], 1)
            pe.wait_ge(S["io_landed"], 32)
            yv = y[:].rearrange("p a b -> p (a b)").rearrange("p (t d) -> p t d", t=TT)
            for m in range(DT):
                if m >= 4:
                    pe.wait_ge(S["x_new"], m - 3)
                for t in range(TT):
                    ins = tr(psum[:, m % 4, t * P:(t + 1) * P], yv[:, t, m * P:(m + 1) * P], ident[:])
                ins.then_inc(S["x_transposed"], 1)
            pe.wait_ge(S["tables_t"], 1)
            for i in range(NTAB):
                ins = tr(psum[:, 5 + i // 16, (i % 16) * NPAIR:(i % 16 + 1) * NPAIR], prow[:, i, :], ident[0:NPAIR, 0:NPAIR])
            ins.then_inc(S["tab_tr"], 1)
            pe.wait_ge(S["x_new"], DT)
            pe.wait_ge(S["const_made"], 3)
            products(0, x_gate("ffn1"), 0)
            products(1, (S["h_ready"], 1))
            total(1)
            total(2)

            pe.wait_ge(S["ssm_landed"], 16 * 6)
            for i in range(4):
                ins = tr(psum[:, 7, i * P:(i + 1) * P], st_rows[:, i // 2, i % 2, :], ident[:])
            ins.then_inc(S["st_tr"], 1)
            stage = ssm_f[:].rearrange("p r j n -> p (r j n)")
            for half in range(2):
                t0 = half * HT
                for ri in range(2):
                    pe.wait_ge(S["cz_masked"], 2 * half + ri + 1)
                    if half:
                        pe.wait_ge(S["y_gelu"], HT)
                    for t in range(HT):
                        ins = tr(psum[:, 5 + ri, t * P:(t + 1) * P], stage[:, (ri * HT + t) * P:(ri * HT + t + 1) * P], ident[:])
                    ins.then_inc(S["cz_tr"], 1)
                for s in range(QL):
                    pe.wait_ge(S["zn_ready"], half * QL + s + 1)
                    zn = ssm_tmp[:, s % 2, :].rearrange("p (r n) -> p r n", r=2)
                    for ri in range(2):
                        if s == 0:
                            pe.wait_ge(S["cz_ready"], 2 * half + ri + 1)
                        else:
                            pe.wait_ge(S["z_copied"], (half * QL + s - 1) * 2 + ri + 1)
                        for t in range(HT):
                            ins = tr(psum[:, 5 + ri, t * P:(t + 1) * P], zn[:, ri, t * P:(t + 1) * P], ident[:])
                        ins.then_inc(S["z_tr"], 1)
                    if s == 0:
                        pe.wait_ge(S["st_copied"], 1)
                        pe.wait_ge(S["cz_ready"], 2 * half + 2)
                    if half * QL + s:
                        pe.wait_ge(S["m_ready"], half * QL + s)
                    for t in range(HT):
                        for ri in range(2):
                            ins = mm(psum[:, 7, t * P:(t + 1) * P], zn[:, ri, t * P:(t + 1) * P],
                                     c_z[:, ri, t * P:(t + 1) * P], start=(ri == 0), stop=(ri == 1))
                    ins.then_inc(S["m_mm"], 1)
                pe.wait_ge(S["z_copied"], (half + 1) * QL * 2)
                pe.wait_ge(S["u_ready"], DT)
                if half:
                    pass
                for t2 in range(HT // 2):
                    if half or t2:
                        pe.wait_ge(S["f_copied"], 8 * (half * 2 + t2))
                    for t in range(2):
                        m = t0 + 2 * t2 + t
                        um = ssm_u[:, m, :].rearrange("p (n r) -> p r n", r=QL)
                        for ri in range(2):
                            c = (t * 2 + ri) * NQ
                            for r in range(QL):
                                for j in range(4):
                                    rows = slice(32 * j, 32 * j + 32)
                                    tl = 2 * t2 + t
                                    ins = mm(psum[:, j, c:c + NQ], ssm_t[rows, QL - 1 - r, ri, tl * P:(tl + 1) * P], um[rows, r, :],
                                             start=(r == 0), stop=(r == QL - 1))
                    ins.then_inc(S["f_mm"], 1)
                pe.wait_ge(S["m_ready"], (half + 1) * QL)
                for t in range(HT):
                    m = t0 + t
                    if t >= 2:
                        pe.wait_ge(S["y_gelu"], m - 1)
                    bank = 5 + t % 2
                    um = ssm_u[:, m, :].rearrange("p (n r) -> p r n", r=QL)
                    for r in range(QL):
                        for d in range(r + 1):
                            mm(psum[:, bank, r * NQ:(r + 1) * NQ], ssm_m[:, d, t, :], um[:, r - d, :],
                               start=(r == 0), stop=False, skip_group_check=True)
                    if t == 0:
                        pe.wait_ge(S["g_ready"], half + 1)
                        pe.wait_ge(S["ca_ready"], half + 1)
                    g = ssm_g[:].rearrange("p a b -> p (a b)").rearrange("p (r j n) -> p r j n", r=2, j=HP)
                    for r in range(QL):
                        for ri in range(2):
                            for j in range(4):
                                jl = t * 4 + j
                                ins = mm(psum[32 * j:32 * j + 32, bank, r * NQ:(r + 1) * NQ], ssm_ca[:, r, ri, jl * 32:(jl + 1) * 32],
                                         g[:, ri, jl, :], start=False, stop=(r == QL - 1 and ri == 1), skip_group_check=True)
                    ins.then_inc(S["y_mm"], 1)
            for i in range(4):
                tr(psum[:, 7, i * P:(i + 1) * P], st_out[:].rearrange("p r b j -> p (r b j)")[:, i * P:(i + 1) * P], ident[:])
            for ri in range(2):
                ins = tr(psum[0:NPAIR, TOT, ri * P:(ri + 1) * P], st_prompt[:, ri, :], ident[:])
            ins.then_inc(S["st_tr2"], 1)
            pe.wait_ge(S["sout_ready"], 1)
            products(2, x_gate("glu"))
            total(3)
            products(3, x_gate("ffn2"), 4)
            products(4, (S["h_ready"], FT + 1))
            total(5)
            products(5, x_gate("kv"), 6)
            pe.wait_ge(S["acc_read"], STARTS[6])
            for g in range(2 * DT * TT // 4):
                if g >= 3:
                    pe.wait_ge(S["kv_copied_a" if (g - 3) % 2 else "kv_copied_v"], (g - 3) // 2 + 1)
                for a in range(4):
                    ins = tr(psum[:, 5 + g % 3, a * P:(a + 1) * P], kvT[:, (g % 4) * 4 + a, (g // 4) * P:(g // 4 + 1) * P], ident[:])
                ins.then_inc(S["kv_tr"], 1)
            products(6, x_gate("ffn1b"))
            products(7, (S["h_ready"], 2 * FT + 1))
            total(7)
            products(8, x_gate("q"), 8)

            with pe.Fori(0, NB) as b:
                for kb in range(KB):
                    for g in range(2):
                        if g == 0:
                            pe.wait_ge(k_landed[kb], b * 16 + 16)
                        if kb:
                            pe.wait_ge(S["kt_copied_a" if g else "kt_copied_v"], b * KB + kb)
                        elif g == 0:
                            pe.wait_ge(S["acc_read"], STARTS[9])
                        for a in range(4):
                            c = (g * 4 + a) * P
                            ins = tr(psum[:, 5 + g, a * P:(a + 1) * P], k_raw[:, kb, c:c + P], ident[:])
                        ins.then_inc(S["kt_tr"], 1)
                for n in ("kt_copied_a", "kt_copied_v"):
                    pe.wait_ge(S[n], b * KB + KB)
                pe.wait_ge(S["kn_landed"], b * 16 + 16)
                pe.wait_ge(S["q_ready"], b + 1)
                pe.wait_ge(S["o_ready"], b * 2 + 1)
                for hh in range(2):
                    for a in range(4):
                        lhs = q_blk[:, 4 * hh + a].rearrange("p g i -> p (g i)")
                        rows = slice(32 * a, 32 * a + 32)
                        mm(psum[rows, 2 * hh, :], lhs, kT[:, 4 * hh + a, 0:KC], start=True, stop=True)
                        ins = mm(psum[rows, 2 * hh + 1, 0:LS], lhs, kT[:, 4 * hh + a, KC:KN], start=True, stop=True)
                    ins.then_inc(S["scored"], 1)
                for hh in range(2):
                    pe.wait_ge(S["prob_ready"], b * 2 + (hh + 1))
                    if hh:
                        pe.wait_ge(S["pt_copied"], b * 2 + 1)
                        pe.wait_ge(S["pt4_copied"], b * 2 + 1)
                    for kb in range(KB):
                        tr(psum[:, 7, kb * P:(kb + 1) * P], prob[:, hh, kb * P:(kb + 1) * P], ident[:])
                    tr(psum[0:LS, TOT, 0:P], prob[:, hh, KC:KN], ident[:]).then_inc(S["p_tr"], 1)
                pe.wait_ge(S["v_landed"], b * 32 + 32)
                for hh in range(2):
                    pe.wait_ge(S["pt_copied"], b * 2 + (hh + 1))
                    pe.wait_ge(S["pt4_copied"], b * 2 + (hh + 1))
                    for a in range(4):
                        c = (4 * hh + a) * P
                        for kb in range(KB + 1):
                            n = P if kb < KB else LS
                            ins = mm(psum[:, 2 * hh + 1, P + 32 * a:P + 32 * a + 32], v_raw[0:n, kb, c:c + P],
                                     probT[0:n, hh, kb * P + 32 * a:kb * P + 32 * a + 32], start=(kb == 0), stop=(kb == KB))
                    ins.then_inc(S["pv_done"], 1)
            with pe.Fori(0, DT // 2) as turn:
                jj = turn * 2
                for s in range(2):
                    pe.wait_ge(p_landed[s], jj * 24 + 48)
                    pe.wait_ge(S["qp_ready"], jj + (s + 1))
                    for hh in range(2):
                        rows = slice(hh * HD, (hh + 1) * HD)
                        mm(psum[:, hh, 0:P], q_p[rows, s, 0:P], kTp[rows, s, 0:P], start=True, stop=True)
                        mm(psum[:, hh, P:3 * P], q_p[rows, s, P:2 * P], kTp[rows, s, :], start=True, stop=True).then_inc(S["pscored"], 1)
                    for hh in range(2):
                        pe.wait_ge(S["pprob"], jj * 2 + (2 * s + hh + 1))
                        for a in range(3):
                            ins = tr(psum[:, 2 + hh, a * P:(a + 1) * P], prob_p[:, hh, a * P:(a + 1) * P], ident[:])
                        ins.then_inc(S["pp_tr"], 1)
                    for hh in range(2):
                        rows = slice(hh * HD, (hh + 1) * HD)
                        pe.wait_ge(S["ppt_copied"], jj * 2 + (2 * s + hh + 1))
                        mm(psum[rows, 5 + hh, 0:P], v_p[:, s, 0, rows], probT_p[:, hh, 0:P], start=True, stop=True)
                        mm(psum[rows, 5 + hh, P:2 * P], v_p[:, s, 0, rows], probT_p[:, hh, P:2 * P], start=True, stop=False)
                        mm(psum[rows, 5 + hh, P:2 * P], v_p[:, s, 1, rows], probT_p[:, hh, 2 * P:3 * P], start=False,
                           stop=True).then_inc(S["ppv"], 1)
            products(9, x_gate("o"))
            total(9)
            products(10, x_gate("ffn2b"), 10)
            products(11, (S["h_ready"], 3 * FT + 1))
            total(11)
            for g in range(2 * TT):
                if g < 2:
                    pe.wait_ge(S["x_new"], 6 * DT + 4 * (g + 1))
                if g >= 3:
                    pe.wait_ge(S["out_copied_a" if (g - 3) % 2 else "out_copied_v"], (g - 3) // 2 + 1)
                for a in range(4):
                    m = (g % 2) * 4 + a
                    ins = tr(psum[:, 5 + g % 3, a * P:(a + 1) * P], x[:, m, (g // 2) * P:(g // 2 + 1) * P], ident[:])
                ins.then_inc(S["out_tr"], 1)


_OUTS = [("y_prompt", (1, SEQ, D)), ("y_sample", (NB, LS, D)), ("ssm_re_p", (1, 1, NG, NS)), ("ssm_im_p", (1, 1, NG, NS)),
         ("k_p", (1, SEQ, NH, HD)), ("v_p", (1, SEQ, NH, HD)), ("ssm_re_s", (1, NB, NG, NS)), ("ssm_im_s", (1, NB, NG, NS)),
         ("k_s", (NB, LS, NH, HD)), ("v_s", (NB, LS, NH, HD))]


def kernel(**inputs):
    import numpy as _np
    import concourse.bacc as _bacc
    from concourse.bass_utils import run_bass_kernel_spmd as _run

    nc = _bacc.Bacc("TRN2", target_bir_lowering=False, num_devices=1)
    arrays = {n: _np.ascontiguousarray(a) for n, a in inputs.items() if n != "attn_rel_bias"}
    arrays["bias_reversed"] = _np.ascontiguousarray(_np.asarray(inputs["attn_rel_bias"])[0, :, ::-1])
    i = _np.arange(P)
    arrays["c_ident"] = _np.eye(P, dtype=_np.float32)
    arrays["c_blockmask"] = (i[:, None] // 32 == i[None, :] // 32).astype(_np.float32)
    arrays["c_parmask"] = (i[:, None] // SC % 2 == _np.arange(2)[None, :]).astype(_np.float32)
    A = inputs_of(nc, {n: a.shape for n, a in arrays.items()})
    O = {n: nc.dram_tensor(f"out_{n}_dram", s, F32, kind="ExternalOutput").ap() for n, s in _OUTS}
    scratch = {"bias": nc.dram_tensor("scratch_bias", [NH, PAD + NREL], F32).ap(),
               "tiles": nc.dram_tensor("scratch_tiles", [NH, P, SEQ], F32).ap(),
               "kT": nc.dram_tensor("scratch_kT", [P, DT * TOK], F32).ap(),
               "v": nc.dram_tensor("scratch_v", [TOK, D], F32).ap()}
    build(nc, A, O, scratch)
    r = _run(nc, [{f"in_{n}_dram": a for n, a in arrays.items()}], core_ids=[0])
    return tuple(r.results[0][f"out_{n}_dram"] for n, _ in _OUTS)
```

```python
import math

import numpy as np

import concourse.bass as bass
from concourse import mybir

F32 = mybir.dt.float32
F32R = mybir.dt.float32r
ALU = mybir.AluOpType
ACT = mybir.ActivationFunctionType
AX_X = mybir.AxisListType.X

P = 128
D = 1024
DT = D // P
SEQ = 256
NB = 8
LS = 16
TOK = SEQ + NB * LS
TT = TOK // P
FF = 2816
FT = FF // P
NG = 64
SC = 16
NS = 64
NPAIR = NG // 2
QL = 4
NQ = TOK // QL
NC16 = TOK // LS
PRUNS = SEQ // LS
HP = NPAIR // 2
HT = DT // 2
NH = 16
HD = 64
KC = 512
KB = KC // P
KN = KC + LS
NREL = 257
PAD = 128
EPS = 1e-6
SCALE = HD ** -0.5
NEG = -1e30
TWO_PI_HI = 6.28125
TWO_PI_LO = 2 * math.pi - TWO_PI_HI
ROUND = 1.5 * 2 ** 23

STAGES = [("in", 22), ("out", 8), ("glu", 8), ("in", 22), ("out", 8), ("kv", 8),
          ("in", 22), ("out", 8), ("q", 4), ("o", 4), ("in", 22), ("out", 8)]
STARTS = [sum(c for _, c in STAGES[:i]) for i in range(len(STAGES) + 1)]
CHUNKS = STARTS[-1]
SLOT = FT * P

(PZ, PA, A4S, A16S) = (0, 8, 16, 18)
A16 = 20
LR, LI, DL, TH, MAG, SIN, ANG, COS, W0, W1, W2, W3 = range(22, 34)
NTAB = 22


def inputs_of(nc, shapes):
    return {n: nc.dram_tensor(f"in_{n}_dram", s, F32, kind="ExternalInput").ap() for n, s in shapes.items()}


class Link:

    def __init__(self, eng, sem):
        self.eng, self.sem, self.n = eng, sem, 0

    def mark(self, ins):
        self.n += 1
        ins.then_inc(self.sem, 1)
        return self.n

    def settle(self, n=None):
        self.eng.wait_ge(self.sem, self.n if n is None else n)

    def __call__(self, ins):
        self.mark(ins)
        self.settle()


def build(nc, A, O, scratch):
    base = 16512
    place = {"at": base}

    def sb(name, shape, dt=F32, at=None):
        size = 4 * int(np.prod(shape[1:]))
        if at is None:
            at = place["at"]
            place["at"] += (size + 31) // 32 * 32
        return nc.alloc_sbuf_tensor_at(name, shape, dt, offset=at)

    x = sb("x", [P, DT, TOK])
    Y_AT = place["at"]
    y = sb("y", [P, DT, TOK])
    w_at = place["at"]
    w_raw = [sb(f"w_raw{s}", [P, SLOT]) for s in range(2)]
    w_hi = [sb(f"w_hi{s}", [P, SLOT], F32R) for s in range(2)]
    w_lo = [sb(f"w_lo{s}", [P, SLOT], F32R) for s in range(2)]
    ident = sb("ident", [P, P])
    ones = sb("ones", [P, P])
    parmask = sb("parmask", [P, 2])
    consts = sb("consts", [P, 4])
    gains = sb("gains", [P, 104])
    half_gains = sb("half_gains", [P, 96])
    norm_temps = place["at"]
    ssum = sb("ssum", [P, TOK])
    sq = sb("sq", [P, 2, TOK])
    std = sb("std", [P, TOK])
    rstd = sb("rstd", [P, TOK])
    scaled = sb("scaled", [P, 2, TOK])
    ffn_temps = place["at"]
    gate_s = sb("gate_s", [P, TOK])
    up_s = sb("up_s", [P, TOK])
    act_s = sb("act_s", [P, TOK])
    h_full = sb("h_full", [P, TOK])
    tab = sb("tab", [P, NTAB, NPAIR])
    R = place["at"]
    x_hi = sb("x_hi", [P, DT, TOK], F32R)
    x_lo = sb("x_lo", [P, DT, TOK], F32R)
    h_hi = sb("h_hi", [P, FT, TOK], F32R)
    h_lo = sb("h_lo", [P, FT, TOK], F32R)
    assert place["at"] <= 229344

    def region(plan, skip=0):
        at = R + 4 * skip
        out = []
        for name, shape, dt in plan:
            out.append(sb(name, shape, dt, at=at))
            at += (4 * int(np.prod(shape[1:])) + 31) // 32 * 32
        assert at <= 229344, (at, name)
        return out

    gain_rows, = region([("gain_rows", [104, P], F32)], skip=2 * DT * TOK)
    lam_rows, lstep, table_rev = region([("lam_rows", [NPAIR, 2, P], F32), ("lstep", [NPAIR, 4], F32),
                                         ("table_rev", [NH, PAD + NREL], F32)], skip=2 * (DT + FT) * TOK)
    prow, = region([("prow", [NPAIR, NTAB + 12, P], F32)])
    param_rows = [prow[:, i, :] for i in range(NTAB + 12)]
    param_rows[LR], param_rows[LI] = lam_rows[:, 0, :], lam_rows[:, 1, :]
    (ssm_z, ssm_m, ssm_t, ssm_z2, ssm_f, u_q, b_nat, c_z, c_masked, st_rows) = region([
        ("ssm_z", [P, 2, HP, QL, 32], F32),
        ("ssm_m", [P, HP, QL, 32], F32),
        ("ssm_t", [P, 2, HP, P], F32),
        ("ssm_z2", [P, 2, HP, QL, 32], F32),
        ("ssm_f", [P, HP, 2, NQ], F32),
        ("u_q", [P, NPAIR, NQ], F32),
        ("b_nat", [P, 2, NPAIR, SC], F32),
        ("c_z", [P, 2, 2, HP * 32], F32),
        ("c_masked", [P, 2, 2, NS], F32),
        ("st_rows", [P, 2, 2, P], F32)])
    c_nat = sb("c_nat", [P, 2, DT, NS], at=R + 4 * 2 * HP * QL * 32)
    u_r = sb("u_r", [P, DT, QL, NQ], at=R + 4 * (3 * 4096 + 2048))
    y_r = sb("y_r", [P, DT, QL, NQ], at=R + 4 * (4096 + 2048))
    z_of = [ssm_z, ssm_z2]
    ca_of = z_of
    st_out = sb("st_out", [P, 2, NB, NPAIR], at=ffn_temps)
    st_prompt = sb("st_prompt", [P, 2, NPAIR], at=ffn_temps + 4 * 2 * NB * NPAIR)
    ssm_e0 = sb("ssm_e0", [P, 2, HP, NC16], at=ffn_temps + 4 * 2 * (NB + 1) * NPAIR)
    ca_tmp = sb("ca_tmp", [P, 2, HP * 32], at=norm_temps)
    state_tmp = sb("state_tmp", [P, 2, 2, HP, NC16], at=norm_temps + 4 * 3 * TOK)
    tail = [w_at + 4 * SLOT * i + 4 * DT * 2 * P for i in range(6)]
    d_diag = [sb(f"d_diag{h}", [P, HP, 32], at=tail[2 + h]) for h in range(2)]
    st_in = sb("st_in", [P, 2, NB, NPAIR], at=tail[4])
    ssm_g = y
    gv = y[:].rearrange("p a b -> p (a b)").rearrange("p (r j s q) -> p r j s q", r=2, j=HP, s=NC16)
    kvT = sb("kvT", [P, 2 * DT, TOK], at=229344 - 4 * 2 * DT * TOK)
    k_tok = sb("k_tok", [P, TT, D], at=Y_AT)
    v_tok = sb("v_tok", [P, TT, D], at=229344 - 4 * 3 * DT * TOK)
    qT = y
    k_raw, kT, v_raw, oT = region([("k_raw", [P, KB, D], F32), ("kT", [P, DT, KN], F32), ("v_raw", [P, KB + 1, D], F32),
                                   ("oT", [P, DT, TOK], F32)], skip=2 * DT * TOK)
    bias_s = sb("bias_s", [P, 2, KN], at=ffn_temps)
    prob, probT, q_blk, o_rows, row_s = region([("prob", [P, 2, KN], F32), ("probT", [P, 2, (KB + 1) * P], F32),
                                        ("q_blk", [P, DT, 2, LS], F32), ("o_rows", [P, 2, P], F32), ("row_s", [P, 2, 4], F32)])
    at = R + 2 * 4 * DT * TOK
    kT_p = sb("kT_p", [P, DT, SEQ], at=at)
    v_all = sb("v_all", [P, 2, D], at=at + 4 * DT * SEQ)
    bias_at = at + 4 * KB * D
    bias_p = sb("bias_p", [P, NH, 3 * P], at=bias_at)
    probT_p = sb("probT_p", [P, 2, 3 * P], at=bias_at + 4 * NH * 3 * P)
    v_p = sb("v_p", [P, 2, 2, P], at=bias_at + 4 * (NH + 2) * 3 * P)
    kTp = sb("kTp", [P, 2, SEQ], at=bias_at + 4 * (NH + 2) * 3 * P + 2048)
    prob_p = sb("prob_p", [P, 2, 2, 3 * P], at=ffn_temps)
    q_p = sb("q_p", [P, 2, SEQ], at=ffn_temps + 4 * 4 * TOK)
    row_p = sb("row_p", [P, 2, 2, 6], at=ffn_temps + 4 * (4 * TOK + 2 * SEQ))
    x_out = sb("x_out", [P, TT, D], at=R)

    psum = nc.alloc_psum_tensor("psum", [P, 8, 512], F32)
    TOT = 4

    def acc(s, h):
        return psum[:, s + 2 * h, 0:TOK]

    names = """const_landed io_landed const_made gain_rows_t tables_t gains_ready w_hi_ready w_lo_ready chunk_done
        acc_read x_transposed x_new x_hi_ready x_lo_ready squared sq_added total_ready std_ready rstd_ready exp_in
        sin_in scaled_ready gate_scaled silu_ready h_full_ready h_ready sig_ready kv_tr kv_copied_v kv_copied_a
        stored ssm_landed u_landed y_landed kvp_landed d_ready m_zeroed z_zeroed rows_made rows_raw tab_tr u_scaled u_ready
        cz_masked cz_tr cz_ready zn_ready z_tr z_copied m_mm m_ready ca_ready f_mm f_copied st_tr st_copied g_ready
        y_mm y_gelu st_tr2 sout_ready trp_made trp_stored bias_landed kn_landed kt_tr kt_copied_v kt_copied_a
        q_ready pt4_copied soft_made recip_made qp_ready vp_ready psoft_made precip_made bias_masked scored soft_in
        exped prob_ready p_tr pt_copied pv_done o_rows_made o_tr o_ready pscored psoft pexped pprob pp_tr
        ppt_copied ppv po_ready out_tr out_copied_v out_copied_a dve_link act_link pool_link pe_link""".split()
    S = {n: nc.alloc_semaphore(n) for n in names}
    w_landed = [nc.alloc_semaphore(f"w_landed{s}") for s in range(2)]
    v_landed = [nc.alloc_semaphore(f"v_landed{s}") for s in range(2)]
    k_landed = [nc.alloc_semaphore(f"k_landed{s}") for s in range(KB)]
    p_landed = [nc.alloc_semaphore(f"p_landed{s}") for s in range(2)]

    def weight_source(stage, i):
        kind = STAGES[stage][0]
        if kind == "in":
            w = {0: A["ffn1_w_in"][0], 3: A["ffn2_w_in"][0], 6: A["ffn1_w_in"][1], 10: A["ffn2_w_in"][1]}[stage]
        elif kind == "out":
            w = {1: A["ffn1_w_out"][0], 4: A["ffn2_w_out"][0], 7: A["ffn1_w_out"][1], 11: A["ffn2_w_out"][1]}[stage]
        else:
            w = {"glu": A["ssm_w_glu"], "q": A["attn_w_q"], "o": A["attn_w_o"]}[kind][0] if kind != "kv" else A["w_kv"]
        if kind in ("in", "glu"):
            v = w.rearrange("(k p) (h n) -> h p k n", p=P, h=2)
            return [v[h][:, :, bass.ts(i, P)] for h in range(2)]
        v = w.rearrange("(k p) n -> p k n", p=P)
        if kind == "out":
            return [v[:, h * (FT // 2):(h + 1) * (FT // 2), bass.ts(i, P)] for h in range(2)]
        return [v[:, h * (DT // 2):(h + 1) * (DT // 2), bass.ts(i, 2 * P)] for h in range(2)]

    def weight_slot(t, kind):
        if kind == "out":
            v = t[:, 0:FT * P].rearrange("p (k c) -> p k c", c=P)
            return [v[:, h * (FT // 2):(h + 1) * (FT // 2)] for h in range(2)]
        v = t[:, 0:DT * 2 * P].rearrange("p (k n) -> p k n", n=2 * P)
        if kind in ("in", "glu"):
            return [v[:, :, h * P:(h + 1) * P] for h in range(2)]
        return [v[:, h * (DT // 2):(h + 1) * (DT // 2)] for h in range(2)]

    def slot_size(kind):
        return FT * P if kind == "out" else DT * 2 * P

    def gain(col):
        return gains[:, col:col + 1]

    def gain_col(layer, n, m):
        return (layer * 6 + n) * DT + m

    SPLITS = [gain_col(0, 0, 0), gain_col(0, 4, 0), 96, gain_col(1, 0, 0), gain_col(1, 2, 0), gain_col(1, 4, 0)]
    ORDER = ["ffn1", "glu", "ffn2", "kv", "ffn1b", "q", "o", "ffn2b"]
    split_base = {n: DT * i for i, n in enumerate(ORDER)}
    NORMS = 12

    def kv_dst(g):
        return (v_tok if g % 4 >= 2 else k_tok)[:, g // 4, (g % 2) * 512:(g % 2 + 1) * 512]

    def out_dst(g):
        return x_out[:, g // 2, (g % 2) * 512:(g % 2 + 1) * 512]

    with nc.Block() as block:

        @block.sync
        def _(sp):
            def load(dst, src, sem):
                sp.dma_start(dst, src).then_inc(sem, 16)

            load(ident[:], A["c_ident"], S["const_landed"])
            load(parmask[:], A["c_parmask"], S["const_landed"])
            yv = y[:].rearrange("p a b -> p (a b)").rearrange("p (t d) -> p t d", t=TT)
            load(yv[:, 0:2, :], A["x_prompt"][0].rearrange("(t p) d -> p t d", p=P), S["io_landed"])
            load(yv[:, 2, :], A["x_sample"].rearrange("b l d -> (b l) d"), S["io_landed"])
            load(gain_rows[0:96, :], A["norm_gains"].rearrange("l n (t c) -> (l n t) c", c=P), S["const_landed"])
            load(gain_rows[96:104, :], A["kv_norm"].rearrange("(t c) -> t c", c=P), S["const_landed"])
            load(lam_rows[:, 0, :], A["ssm_lambda_re"][0].rearrange("(j g) s -> j (g s)", g=2), S["rows_raw"])
            load(lam_rows[:, 1, :], A["ssm_lambda_im"][0].rearrange("(j g) s -> j (g s)", g=2), S["rows_raw"])
            load(lstep[:, 0:2], A["ssm_log_step"][0].rearrange("(j g) -> j g", g=2), S["rows_raw"])
            load(table_rev[:, PAD:], A["bias_reversed"], S["rows_raw"])

            def weights(stage, first=0, last=None):
                kind, count = STAGES[stage]
                last = count if last is None else last

                def one(i, s, n, wait):
                    if wait:
                        sp.wait_ge(S["w_lo_ready"], n - 1)
                    for dst, src in zip(weight_slot(w_raw[s], kind), weight_source(stage, i)):
                        sp.dma_start(dst, src).then_inc(w_landed[s], 16)

                n0 = STARTS[stage]
                if n0 + first < 2:
                    for i in range(2):
                        one(i, i, n0 + i, False)
                    first = 2
                if first < last:
                    with sp.Fori(first // 2, last // 2) as turn:
                        i = turn * 2
                        for s in range(2):
                            one(i + s, s, i + (n0 + s), True)

            weights(0, 0, 2)
            sp.wait_ge(S["trp_made"], 1)
            sp.dma_start(scratch["bias"], table_rev[:]).then_inc(S["trp_stored"], 16)
            sp.wait_ge(S["trp_stored"], 16)
            skew = bass.AP(tensor=scratch["bias"].tensor, offset=PAD, ap=[[PAD + NREL, NH], [-1, P], [1, SEQ]])
            sp.dma_start(scratch["tiles"], skew).then_inc(S["trp_stored"], 16)
            weights(0, 2)
            weights(1)
            weights(2, 0, 4)
            sp.wait_ge(S["chunk_done"], STARTS[2])
            load(b_nat[:, 0], A["ssm_b_re"][0].rearrange("(j g) s c -> (g s) j c", g=2), S["ssm_landed"])
            load(b_nat[:, 1], A["ssm_b_im"][0].rearrange("(j g) s c -> (g s) j c", g=2), S["ssm_landed"])
            load(c_nat[:, 0], A["ssm_c_re"][0].rearrange("(t g) c s -> (g c) t s", g=8), S["ssm_landed"])
            load(c_nat[:, 1], A["ssm_c_im"][0].rearrange("(t g) c s -> (g c) t s", g=8), S["ssm_landed"])
            for ri, n in enumerate(("state_ssm_re", "state_ssm_im")):
                load(st_rows[:, ri], A[n][0].rearrange("(t b) (j g) s -> (b j) t (g s)", t=2, g=2), S["ssm_landed"])
            for h in range(2):
                src = bass.AP(tensor=A["ssm_d"].tensor, offset=h * D // 2, ap=[[0, 32], [1, D // 2]])
                load(d_diag[h][P - 32:P].rearrange("p j c -> p (j c)"), src, S["ssm_landed"])
            sp.wait_ge(S["u_ready"], DT)
            uq = u_q[:].rearrange("p (t j) n -> p t j n", j=4)
            for r in range(QL):
                for j in range(4):
                    load(uq[32 * r:32 * r + 32, :, j, :], u_r[32 * j:32 * j + 32, :, r, :], S["u_landed"])
            for h in range(2):
                ts = slice(h * HT, (h + 1) * HT)
                sp.wait_ge(S["y_gelu"], (h + 1) * HT)
                for r in range(QL):
                    for j in range(4):
                        load(y_r[32 * j:32 * j + 32, ts, r, :], uq[32 * r:32 * r + 32, ts, j, :], S["y_landed"])
            sp.wait_ge(S["sout_ready"], 1)
            for ri, n in enumerate(("ssm_re_s", "ssm_im_s")):
                sp.dma_start(O[n][0].rearrange("(t b) (j g) s -> (b j) t (g s)", t=2, g=2), st_rows[:, ri]).then_inc(S["stored"], 16)
            for ri, n in enumerate(("ssm_re_p", "ssm_im_p")):
                sp.dma_start(O[n][0, 0].rearrange("(j g) s -> j (g s)", g=2), c_masked[0:NPAIR, ri]).then_inc(S["stored"], 16)
            weights(2, 4)
            weights(3)
            weights(4)
            weights(5)
            weights(6, 0, 4)
            sp.wait_ge(S["kv_copied_v"], DT * TT // 4)
            sp.wait_ge(S["kv_copied_a"], DT * TT // 4)
            kvo = [k_tok, v_tok]
            for w, (np_, ns_) in enumerate((("k_p", "k_s"), ("v_p", "v_s"))):
                sp.dma_start(O[np_][0].rearrange("(t p) h d -> p t (h d)", p=P), kvo[w][:, 0:2]).then_inc(S["stored"], 16)
                sp.dma_start(O[ns_].rearrange("b l h d -> (b l) (h d)"), kvo[w][:, 2]).then_inc(S["stored"], 16)
            sp.dma_start(scratch["v"].rearrange("(t p) d -> p t d", p=P), kvo[1][:]).then_inc(S["stored"], 16)
            sp.dma_start(scratch["kT"].rearrange("p (m t) -> p m t", m=DT), kvT[:, 0:DT, :]).then_inc(S["stored"], 16)
            weights(6, 4)
            weights(7)
            weights(8)
            sp.wait_ge(S["stored"], 16 * 10)
            sp.wait_ge(S["trp_stored"], 32)
            sp.wait_ge(S["chunk_done"], STARTS[8])
            tb = scratch["tiles"]
            ks = A["cache_k"].rearrange("b (t p) h d -> (b t) p (h d)", p=P)
            vs = A["cache_v"].rearrange("b (t p) h d -> b p t (h d)", p=P)
            kTs = scratch["kT"].rearrange("p (m t) -> p m t", m=DT)

            def load_k(b, first=False):
                for kb in range(KB):
                    if not first:
                        sp.wait_ge(S["kt_tr"], b * 8 + (2 * kb - 6))
                    sp.dma_start(k_raw[:, kb, :], ks[bass.ds(b * KB + kb, 1)].rearrange("o p d -> (o p) d")).then_inc(k_landed[kb], 16)

            def load_new_k(b, first=False):
                if not first:
                    sp.wait_ge(S["scored"], b * 2)
                sp.dma_start(kT[:, :, KC:KN], kTs[:, :, bass.ds(b * LS + SEQ, LS)]).then_inc(S["kn_landed"], 16)

            def load_v(b, first=False):
                for hh in range(2):
                    cols = slice(hh * 512, (hh + 1) * 512)
                    if not first:
                        sp.wait_ge(S["pv_done"], b * 2 + (hh - 1))
                    sp.dma_start(v_raw[:, 0:KB, cols], vs[bass.ds(b, 1), :, :, cols].rearrange("o p t d -> (o p) t d")).then_inc(v_landed[hh], 16)
                    sp.dma_start(v_raw[0:LS, KB, cols], scratch["v"][bass.ds(b * LS + SEQ, LS), cols]).then_inc(v_landed[hh], 16)

            load_k(0, True)
            load_new_k(0, True)
            for h in range(NH):
                load(bias_s[(h % 8) * LS:(h % 8 + 1) * LS, h // 8, 384:KN], tb[h, 0:LS, 0:KN - 384], S["bias_landed"])
            load_v(0, True)
            weights(9)
            load_k(1)
            with sp.Fori(1, NB - 1) as b:
                load_new_k(b)
                load_k(b + 1)
                load_v(b)
            load_new_k(NB - 1)
            load_v(NB - 1)
            sp.wait_ge(S["kt_tr"], 8 * NB)
            load(kT_p[:], kTs[:, :, 0:SEQ], S["kvp_landed"])
            load(v_all[:], scratch["v"][0:SEQ, :].rearrange("(t p) d -> p t d", p=P), S["kvp_landed"])
            for part, (name, count) in enumerate((("scored", 2 * NB), ("pv_done", 2 * NB))):
                sp.wait_ge(S[name], count)
                hs = slice(part * NH // 2, (part + 1) * NH // 2)
                load(bias_p[:, hs, 0:P], tb[hs, :, P:2 * P].rearrange("h r k -> r h k"), p_landed[part])
                load(bias_p[:, hs, P:3 * P], tb[hs].rearrange("h r k -> r h k"), p_landed[part])
            weights(10)
            weights(11)
            ov = x_out[:]
            for t in range(TT):
                sp.wait_ge(S["out_copied_v"], t + 1)
                sp.wait_ge(S["out_copied_a"], t + 1)
                dst = O["y_prompt"][0, t * P:(t + 1) * P] if t < 2 else O["y_sample"].rearrange("b l d -> (b l) d")
                sp.dma_start(dst, ov[:, t]).then_inc(S["stored"], 16)
            sp.wait_ge(S["stored"], 16 * 13)

        @block.scalar
        def _(act):
            link = Link(act, S["act_link"])

            def split_hi(s, n, kind, wait_used):
                act.wait_ge(w_landed[s], ((n - s) * 16) + 32)
                if wait_used:
                    act.wait_ge(S["chunk_done"], n - 1)
                z = slot_size(kind)
                act.activation(w_hi[s][:, 0:z], w_raw[s][:, 0:z], ACT.Copy).then_inc(S["w_hi_ready"], 1)

            def steps(stage, evacuate, then_root=False):
                kind, count = STAGES[stage]
                n0 = STARTS[stage]
                if count > 2:
                    with act.Fori(0, (count - 2) // 2) as turn:
                        i = turn * 2
                        for s in range(2):
                            evacuate(i + s, s, i + (n0 + s))
                            split_hi(s, i + (n0 + s + 2), kind, True)
                for s in range(2):
                    if then_root and s:
                        act.activation(consts[:, 3:4], consts[:, 0:1], ACT.Sqrt)
                    evacuate(count - 2 + s, s, n0 + count - 2 + s)
                    if stage + 1 < len(STAGES):
                        split_hi(s, n0 + count + s, STAGES[stage + 1][0], True)

            def square(src, n, s):
                if not isinstance(n, int) or n >= 2:
                    act.wait_ge(S["sq_added"], n - 1)
                act.activation(sq[:, s, :], src, ACT.Square).then_inc(S["squared"], 1)

            def root(j):
                act.wait_ge(S["total_ready"], j + 1)
                if j:
                    act.wait_ge(S["rstd_ready"], j)
                act.activation(std[:], psum[:, TOT, 0:TOK], ACT.Sqrt, bias=consts[:, 0:1], scale=1.0 / D).then_inc(S["std_ready"], 1)

            def split_x(name, col, xn0, norm):
                for m in range(DT):
                    act.wait_ge(S["x_new"], xn0 + m + 1)
                    act.activation(x_hi[:, m, :], x[:, m, :], ACT.Copy, scale=gain(col + m)).then_inc(S["x_hi_ready"], 1)
                    if norm is not None:
                        square(x[:, m, :], norm * DT + m, m % 2)

            def silu_step(t):
                def f(i, s, n):
                    act.wait_ge(S["gate_scaled"], i + (t * FT + 1))
                    act.activation(act_s[:], gate_s[:], ACT.Silu).then_inc(S["silu_ready"], 1)
                return f

            def out_step(norm):
                def f(m, s, n):
                    act.wait_ge(S["acc_read"], n + 1)
                    square(y[:, bass.ds(m, 1), :] if not isinstance(m, int) else y[:, m:m + 1, :], m + norm * DT, s)
                return f

            def glu_step(norm):
                def f(m, s, n):
                    act.wait_ge(S["chunk_done"], n + 1)
                    act.activation(act_s[:], acc(s, 1), ACT.Sigmoid).then_inc(S["sig_ready"], 1)
                    out_step(norm)(m, s, n)
                return f

            def o_step(norm):
                def f(i, s, n):
                    act.wait_ge(S["acc_read"], n + 1)
                    for h in range(2):
                        square(y[:, bass.ds(i * 2 + h, 1), :] if not isinstance(i, int) else y[:, 2 * i + h:2 * i + h + 1, :],
                               i * 2 + (norm * DT + h), h)
                return f

            def nothing(i, s, n):
                pass

            act.wait_ge(S["const_made"], 3)
            split_hi(0, 0, "in", False)
            act.wait_ge(S["gains_ready"], 1)
            split_x("ffn1", SPLITS[0], 0, 0)
            split_hi(1, 1, "in", False)
            root(0)
            steps(0, silu_step(0))
            row = param_rows
            act.wait_ge(S["rows_raw"], 64)
            act.activation(lstep[:, 2:4], lstep[:, 0:2], ACT.Exp).then_inc(S["rows_made"], 1)
            act.wait_ge(S["exp_in"], 1)
            act.activation(row[MAG], row[DL], ACT.Exp).then_inc(S["rows_made"], 1)
            act.wait_ge(S["sin_in"], 1)
            act.activation(row[SIN], row[TH], ACT.Sin).then_inc(S["rows_made"], 1)
            link(act.activation(row[ANG], row[TH], ACT.Abs))
            act.activation(row[COS], row[ANG], ACT.Sin, bias=consts[0:NPAIR, 1:2], scale=-1.0).then_inc(S["rows_made"], 1)
            steps(1, out_step(1), True)
            root(1)
            for m in range(DT):
                act.wait_ge(S["x_new"], DT + m + 1)
                square(x[:, m, :], 2 * DT + m, m % 2)
            root(2)
            for m in range(DT):
                act.wait_ge(S["u_scaled"], m + 1)
                act.activation(u_r[:, m], scaled[:, m % 2, :].rearrange("p (n r) -> p r n", r=QL), ACT.Copy,
                               scale=gain(gain_col(0, 2, m))).then_inc(S["u_ready"], 1)
            act.wait_ge(S["st_tr"], 1)
            act.activation(st_in[:].rearrange("p r b j -> p (r b j)"), psum[:, 7, :], ACT.Copy).then_inc(S["st_copied"], 1)
            for half in range(2):
                for ri in range(2):
                    act.wait_ge(S["cz_tr"], 2 * half + ri + 1)
                    act.activation(c_z[:, half, ri, :], psum[:, 5 + ri, :], ACT.Copy, scale=(1.0, -1.0)[ri]).then_inc(S["cz_ready"], 1)

            def copy_t(half):
                for i in range(2 * HT):
                    act.wait_ge(S["z_tr"], half * 2 * HT + i + 1)
                    if half:
                        act.wait_ge(S["f_mm"], 2 * HT)
                    act.activation(ssm_t[:, i // HT, (i % HT) * 4:(i % HT) * 4 + 4, :].rearrange("p j n -> p (j n)"),
                                   psum[:, 4 + (half * 2 * HT + i) % 3, :], ACT.Copy).then_inc(S["z_copied"], 1)

            def spread_m(half):
                act.wait_ge(S["m_mm"], half + 1)
                act.wait_ge(S["m_zeroed"], 1)
                if half:
                    act.wait_ge(S["y_mm"], HT)
                for d in range(QL):
                    b = 32 * (QL - 1 - d)
                    for r in range(QL - d):
                        ins = act.activation(ssm_m[32 * r:32 * r + 32, :, r + d, :],
                                             psum[b:b + 32, 7, :].rearrange("p (j c) -> p j c", c=32), ACT.Copy)
                        if (d, r) != (QL - 1, 0):
                            link.mark(ins)
                link.settle()
                ins.then_inc(S["m_ready"], 1)

            def copy_f(half):
                for i in range(HP // 2):
                    n = half * HP // 2 + i
                    if half:
                        act.wait_ge(S["g_ready"], 1)
                    act.wait_ge(S["f_mm"], n + 1)
                    act.activation(ssm_f[:, 2 * i:2 * i + 2].rearrange("p j r n -> p (j r n)"), psum[:, n % 4, 0:4 * NQ],
                                   ACT.Copy).then_inc(S["f_copied"], 1)

            def gelu(half):
                for t in range(HT):
                    m = half * HT + t
                    act.wait_ge(S["y_mm"], m + 1)
                    act.activation(u_q[:, 4 * m:4 * m + 4, :].rearrange("p j n -> p (j n)"), psum[:, 5 + m % 2, 0:4 * NQ],
                                   ACT.Gelu_apprx_tanh).then_inc(S["y_gelu"], 1)

            copy_t(0)
            copy_f(0)
            spread_m(0)
            copy_t(1)
            copy_f(1)
            gelu(0)
            spread_m(1)
            gelu(1)
            act.wait_ge(S["st_tr2"], 1)
            link(act.activation(st_rows[:].rearrange("p r t n -> p (r t n)"), psum[:, 7, :], ACT.Copy))
            act.activation(c_masked[0:NPAIR].rearrange("p r g n -> p (r g n)"), psum[0:NPAIR, 4, 0:2 * P], ACT.Copy).then_inc(S["sout_ready"], 1)
            act.wait_ge(S["y_landed"], 16 * 4 * QL * 2)
            for m in range(DT):
                act.activation(x_hi[:, m, :].rearrange("p (n r) -> p r n", r=QL), y_r[:, m], ACT.Copy).then_inc(S["x_hi_ready"], 1)
            steps(2, glu_step(3))
            root(3)
            split_x("ffn2", SPLITS[1], 2 * DT, 4)
            root(4)
            steps(3, silu_step(1))
            steps(4, out_step(5), True)
            root(5)
            split_x("kv", SPLITS[2], 3 * DT, 6)
            root(6)
            steps(5, nothing)
            act.wait_ge(S["chunk_done"], STARTS[6])
            for m in range(DT):
                act.activation(x_hi[:, m, :], x[:, m, :], ACT.Copy, scale=gain(SPLITS[3] + m)).then_inc(S["x_hi_ready"], 1)
            for g in range(2 * DT * TT // 4):
                if g % 2:
                    act.wait_ge(S["kv_tr"], g + 1)
                    act.activation(kv_dst(g), psum[:, 5 + g % 3, :], ACT.Copy).then_inc(S["kv_copied_a"], 1)
            steps(6, silu_step(2))
            steps(7, out_step(7), True)
            root(7)
            split_x("q", SPLITS[4], 4 * DT, 8)
            root(8)
            steps(8, nothing)
            def copy_kt(b, kb):
                act.wait_ge(S["kt_tr"], b * 8 + (2 * kb + 2))
                act.activation(kT[:, 4:8, kb * P:(kb + 1) * P], psum[:, 5 + 2 * (kb % 2), :].rearrange("p (a c) -> p a c", c=P),
                               ACT.Copy).then_inc(S["kt_copied_a"], 1)

            def stream(b, more):
                for hh in range(2):
                    act.wait_ge(S["soft_in"], b * 2 + (hh + 1))
                    act.activation(prob[:, hh, :], prob[:, hh, :], ACT.Exp, bias=row_s[:, hh, 0:1],
                                   accum_out=row_s[:, hh, 1:2]).then_inc(S["exped"], 1)
                    if more:
                        act.wait_ge(S["scored"], b * 2 + 2)
                        copy_kt(b + 1, hh)
                if more:
                    copy_kt(b + 1, 2)
                for hh in range(2):
                    act.wait_ge(S["p_tr"], b * 2 + (hh + 1))
                    act.activation(probT[:, hh, 0:KC], psum[:, 2 * hh, :], ACT.Copy).then_inc(S["pt_copied"], 1)
                if more:
                    copy_kt(b + 1, 3)

            for kb in range(KB):
                copy_kt(0, kb)
            with act.Fori(0, NB - 1) as b:
                stream(b, True)
            stream(NB - 1, False)

            def copy_q(j, s):
                act.activation(kTp[:, s:s + 1, :], kT_p[:, bass.ds(j, 1), :], ACT.Copy)
                act.activation(q_p[:, s:s + 1, :], qT[:, bass.ds(j, 1), 0:SEQ], ACT.Copy).then_inc(S["qp_ready"], 1)

            def copy_v(j, s):
                act.activation(v_p[:, s], v_all[:, :, bass.ds(j * P, P)], ACT.Copy).then_inc(S["vp_ready"], 1)

            def exps(j, s):
                for hh in range(2):
                    act.wait_ge(S["psoft"], j * 2 + (hh + 1))
                    for T in range(2):
                        c0, c1 = ((0, P), (P, 3 * P))[T]
                        ins = act.activation(prob_p[:, s, hh, c0:c1], prob_p[:, s, hh, c0:c1], ACT.Exp, bias=row_p[:, s, hh, T:T + 1],
                                             accum_out=row_p[:, s, hh, 2 + T:3 + T])
                    ins.then_inc(S["pexped"], 1)

            def pair(j, s, more, more_q):
                if more_q:
                    act.wait_ge(S["pscored"], j * 2 + 2)
                    copy_q(j + 2, s)
                if more:
                    exps(j + 1, 1 - s)
                for hh in range(2):
                    act.wait_ge(S["pp_tr"], j * 2 + (hh + 1))
                    act.activation(probT_p[:, hh, :], psum[:, 4 + hh, 0:3 * P], ACT.Copy).then_inc(S["ppt_copied"], 1)
                for hh in range(2):
                    rows = slice(hh * HD, (hh + 1) * HD)
                    act.wait_ge(S["ppv"], j * 2 + (hh + 1))
                    act.activation(oT[rows, bass.ds(j, 1), 0:SEQ], psum[rows, 6 + hh, 0:SEQ].unsqueeze(1), ACT.Copy).then_inc(S["po_ready"], 1)
                if more_q:
                    copy_v(j + 2, s)

            act.wait_ge(S["kvp_landed"], 32)
            act.wait_ge(S["pv_done"], 2 * NB)
            for s in range(2):
                copy_q(s, s)
                copy_v(s, s)
            exps(0, 0)
            with act.Fori(0, DT // 2 - 1) as turn:
                for s in range(2):
                    pair(turn * 2 + s, s, True, True)
            pair(DT - 2, 0, True, False)
            pair(DT - 1, 1, False, False)
            act.wait_ge(S["po_ready"], 2 * DT)
            for m in range(DT):
                act.activation(x_hi[:, m, :], oT[:, m, :], ACT.Copy).then_inc(S["x_hi_ready"], 1)
            steps(9, o_step(9), True)
            root(9)
            split_x("ffn2b", SPLITS[5], 5 * DT, 10)
            root(10)
            steps(10, silu_step(3))
            steps(11, out_step(11), True)
            root(11)
            for g in range(2 * TT):
                if g % 2:
                    act.wait_ge(S["out_tr"], g + 1)
                    act.activation(out_dst(g), psum[:, 5 + g % 3, :], ACT.Copy).then_inc(S["out_copied_a"], 1)


        @block.vector
        def _(dve):
            link = Link(dve, S["dve_link"])
            tt, stt, ts = dve.tensor_tensor, dve.scalar_tensor_tensor, dve.tensor_scalar

            def split_lo(s, n, kind):
                z = slot_size(kind)
                dve.wait_ge(S["w_hi_ready"], n + 1)
                tt(w_lo[s][:, 0:z], w_raw[s][:, 0:z], w_hi[s][:, 0:z].bitcast(F32), ALU.subtract).then_inc(S["w_lo_ready"], 1)

            def steps(stage, evacuate, first_steps=()):
                kind, count = STAGES[stage]
                n0 = STARTS[stage]
                for i, more in enumerate(first_steps):
                    evacuate(i, i % 2, n0 + i)
                    split_lo(i % 2, n0 + i + 2, kind)
                    more()
                if count > 2:
                    with dve.Fori(len(first_steps) // 2, (count - 2) // 2) as turn:
                        i = turn * 2
                        for s in range(2):
                            evacuate(i + s, s, i + (n0 + s))
                            split_lo(s, i + (n0 + s + 2), kind)
                for s in range(2):
                    evacuate(count - 2 + s, s, n0 + count - 2 + s)
                    if stage + 1 < len(STAGES):
                        split_lo(s, n0 + count + s, STAGES[stage + 1][0])

            def tile(t, m):
                return t[:, m, :] if isinstance(m, int) else t[:, bass.ds(m, 1), :]

            def root(j):
                dve.wait_ge(S["std_ready"], j + 1)
                dve.reciprocal(rstd[:], std[:]).then_inc(S["rstd_ready"], 1)
                dve.wait_ge(S["rstd_ready"], j + 1)

            def in_step(t):
                def f(i, s, n):
                    c = t * FT + 1
                    dve.wait_ge(S["chunk_done"], n + 1)
                    tt(gate_s[:], acc(s, 0), rstd[:], ALU.mult).then_inc(S["gate_scaled"], 1)
                    tt(up_s[:], acc(s, 1), rstd[:], ALU.mult).then_inc(S["acc_read"], 1)
                    dve.wait_ge(S["acc_read"], n + 1)
                    dve.wait_ge(S["silu_ready"], i + c)
                    tt(h_full[:], act_s[:], up_s[:], ALU.mult).then_inc(S["h_full_ready"], 1)
                    tt(tile(h_hi, i), act_s[:], up_s[:], ALU.mult).then_inc(S["h_full_ready"], 1)
                    dve.wait_ge(S["h_full_ready"], i * 2 + 2 * c)
                    tt(tile(h_lo, i), h_full[:], tile(h_hi, i).bitcast(F32), ALU.subtract).then_inc(S["h_ready"], 1)
                    dve.wait_ge(S["h_ready"], i + c)
                return f

            def out_step(m, s, n):
                dve.wait_ge(S["chunk_done"], n + 1)
                dve.tensor_copy(tile(y, m), acc(s, 0)).then_inc(S["acc_read"], 1)

            def glu_step(m, s, n):
                dve.wait_ge(S["chunk_done"], n + 1)
                dve.wait_ge(S["sig_ready"], m + 1)
                tt(tile(y, m), acc(s, 0), act_s[:], ALU.mult).then_inc(S["acc_read"], 1)

            def o_step(i, s, n):
                dve.wait_ge(S["chunk_done"], n + 1)
                dve.tensor_copy(tile(y, i * 2), acc(s, 0))
                dve.tensor_copy(tile(y, i * 2 + 1), acc(s, 1)).then_inc(S["acc_read"], 1)

            def scaled_step(dst):
                def f(i, s, n):
                    dve.wait_ge(S["chunk_done"], n + 1)
                    tt(tile(dst, i * 2), acc(s, 0), rstd[:], ALU.mult)
                    tt(tile(dst, i * 2 + 1), acc(s, 1), rstd[:], ALU.mult).then_inc(S["acc_read"], 1)
                return f

            def advance(table, col, k, split=None, scol=None):
                for m in range(DT + 1):
                    if m < DT:
                        if m >= 2:
                            dve.wait_ge(S["x_new"], DT * (k + 1) + m - 1)
                        tt(scaled[:, m % 2, :], y[:, m, :], rstd[:], ALU.mult).then_inc(S["scaled_ready"], 1)
                        dve.wait_ge(S["scaled_ready"], DT * k + m + 1)
                        stt(x[:, m, :], scaled[:, m % 2, :], table[:, col + m:col + m + 1], x[:, m, :], ALU.mult,
                            ALU.add).then_inc(S["x_new"], 1)
                    if split is not None and m >= 1:
                        lo(split, scol, m - 1)

            def lo(name, scol, m):
                dve.wait_ge(S["x_hi_ready"], split_base[name] + m + 1)
                stt(x_lo[:, m, :], x[:, m, :], gain(scol + m), x_hi[:, m, :].bitcast(F32), ALU.mult,
                    ALU.subtract).then_inc(S["x_lo_ready"], 1)

            dve.wait_ge(S["gain_rows_t"], 1)
            dve.tensor_copy(gains[:], psum[:, 7, 0:104]).then_inc(S["gains_ready"], 1)
            dve.wait_ge(S["gains_ready"], 1)
            link(ts(half_gains[:], gains[:, 0:96], 0.5, None, ALU.mult))
            for m in range(DT + 1):
                if m < DT:
                    dve.wait_ge(S["x_transposed"], m + 1)
                    dve.tensor_copy(x[:, m, :], psum[:, m % 4, 0:TOK]).then_inc(S["x_new"], 1)
                if m == 3:
                    split_lo(0, 0, "in")
                if m >= 1:
                    lo("ffn1", SPLITS[0], m - 1)
            dve.wait_ge(S["rows_raw"], 64)
            dve.tensor_copy(table_rev[:, 0:PAD], table_rev[:, PAD:PAD + 1].broadcast_to([NH, PAD])).then_inc(S["trp_made"], 1)
            split_lo(1, 1, "in")
            root(0)
            steps(0, in_step(0))
            row = param_rows

            def mul(o, a, b):
                link.mark(tt(row[o], row[a], row[b], ALU.mult))

            def cmul(o, a, b):
                mul(W0, a, b)
                mul(W1, a + 1, b + 1)
                mul(W2, a, b + 1)
                mul(W3, a + 1, b)
                link.settle()
                link.mark(tt(row[o], row[W0], row[W1], ALU.subtract))
                link(tt(row[o + 1], row[W2], row[W3], ALU.add))

            dve.wait_ge(S["chunk_done"], STARTS[1])
            dve.wait_ge(S["rows_made"], 1)
            step = lstep[:, 2:4].unsqueeze(2).broadcast_to([NPAIR, 2, NS])
            two = [r.rearrange("p (g s) -> p g s", g=2) for r in row]
            tt(two[DL], two[LR], step, ALU.mult).then_inc(S["exp_in"], 1)
            link(tt(two[W0], two[LI], step, ALU.mult))
            link(ts(row[W1], row[W0], 1 / (2 * math.pi), ROUND, ALU.mult, ALU.add))
            link(ts(row[W2], row[W1], ROUND, None, ALU.subtract))
            link(stt(row[W1], row[W2], -TWO_PI_HI, row[W0], ALU.mult, ALU.add))
            link(stt(row[W3], row[W2], -TWO_PI_LO, row[W1], ALU.mult, ALU.add))
            ts(row[TH], row[W3], math.pi, -math.pi, ALU.min, ALU.max).then_inc(S["sin_in"], 1)
            dve.wait_ge(S["rows_made"], 4)
            mul(PA, MAG, COS)
            mul(PA + 1, MAG, SIN)
            link.settle()

            def powers():
                cmul(PA + 2, PA, PA)
                cmul(PA + 4, PA + 2, PA)
                cmul(PA + 6, PA + 2, PA + 2)
                cmul(A16, PA + 6, PA + 6)
                cmul(A4S, A16, A16)
                link.mark(dve.tensor_copy(row[A16], row[A4S]))
                link.mark(dve.tensor_copy(row[A16 + 1], row[A4S + 1]))
                link.mark(ts(row[A16S], row[A4S + 1], -1.0, None, ALU.mult))
                link(dve.tensor_copy(row[A16S + 1], row[A4S + 1]))
                link.mark(ts(row[A4S], row[PA + 7], -1.0, None, ALU.mult))
                link.mark(dve.tensor_copy(row[A4S + 1], row[PA + 7]))

            def quotient():
                mul(W0, LR, LR)
                mul(W1, LI, LI)
                link.mark(ts(row[ANG], row[PA], 1.0, None, ALU.subtract))
                link.settle()
                link(tt(row[W2], row[W0], row[W1], ALU.add))
                link(dve.reciprocal(row[DL], row[W2]))
                mul(W0, ANG, LR)
                mul(W1, PA + 1, LI)
                mul(W2, PA + 1, LR)
                mul(W3, ANG, LI)
                link.settle()
                link.mark(tt(row[W0], row[W0], row[W1], ALU.add))
                link(tt(row[W2], row[W2], row[W3], ALU.subtract))
                mul(PZ, W0, DL)
                mul(PZ + 1, W2, DL)
                link.settle()
                cmul(PZ + 2, PZ, PA)
                cmul(PZ + 4, PZ, PA + 2)
                cmul(PZ + 6, PZ, PA + 4)
                dve.tensor_copy(row[W0], row[LR]).then_inc(S["tables_t"], 1)

            steps(1, out_step, (powers, quotient))
            dve.wait_ge(S["tab_tr"], 1)
            link.mark(dve.tensor_copy(tab[:, 0:16, :].rearrange("p a j -> p (a j)"), psum[:, 5, :]))
            link(dve.tensor_copy(tab[:, 16:NTAB, :].rearrange("p a j -> p (a j)"), psum[:, 6, 0:(NTAB - 16) * NPAIR]))
            root(1)
            advance(half_gains, gain_col(0, 1, 0), 0)
            dve.wait_ge(S["x_new"], 2 * DT)
            link.mark(dve.memset(ssm_z[:], 0.0))
            dve.wait_ge(S["ssm_landed"], 16 * 8)
            stage = y[:].rearrange("p a b -> p (a b)")
            zt = [stage[:, 2048 + 256 * i:2304 + 256 * i].rearrange("p (j c) -> p j c", c=SC) for i in range(4)]
            for half in range(2):
                for ri in range(2):
                    src = c_nat[:, ri, half * HT:(half + 1) * HT, :].unsqueeze(2).broadcast_to([P, HT, 2, NS])
                    msk = parmask[:].unsqueeze(1).unsqueeze(3).broadcast_to([P, HT, 2, NS])
                    c = 512 * (2 * half + ri)
                    dst = stage[:, c:c + 512].rearrange("p (t g s) -> p t g s", t=HT, g=2)
                    tt(dst, src, msk, ALU.mult).then_inc(S["cz_masked"], 1)
            last = slice(P - 32, P)
            for half in range(2):
                tt(d_diag[half][last], d_diag[half][last], ident[last, last].unsqueeze(1).broadcast_to([32, HP, 32]),
                   ALU.mult).then_inc(S["d_ready"], 1)

            def build_z(half):
                js = slice(half * HP, (half + 1) * HP)
                if half:
                    dve.wait_ge(S["z_zeroed"], 1)
                for s in range(QL):
                    zn = z_of[half][:, :, :, QL - 1 - s, :].rearrange("p r j (g c) -> p r j g c", g=2)
                    pr, pi = (tab[:, PZ + 2 * s + ri, js].unsqueeze(2).broadcast_to([P, HP, SC]) for ri in range(2))
                    br, bi = (b_nat[:, ri, js, :] for ri in range(2))
                    link.settle()
                    for o, (a, b) in enumerate(((pr, br), (pi, bi), (pr, bi), (pi, br))):
                        link.mark(tt(zt[o], b, a, ALU.mult))
                    link.settle()
                    for g in range(2):
                        rows = slice(g * NS, (g + 1) * NS)
                        link.mark(tt(zn[rows, 0, :, g, :], zt[0][rows], zt[1][rows], ALU.subtract))
                    for g in range(2):
                        rows = slice(g * NS, (g + 1) * NS)
                        ins = tt(zn[rows, 1, :, g, :], zt[2][rows], zt[3][rows], ALU.add)
                        if g == 0 or s < QL - 1:
                            link.mark(ins)
                ins.then_inc(S["zn_ready"], 1)
                dve.wait_ge(S["zn_ready"], half + 1)

            fv = ssm_f[:].rearrange("p j r (s q) -> p r j s q", q=QL)
            t1, t2 = (state_tmp[:, i] for i in range(2))

            def states(half):
                js = slice(half * HP, (half + 1) * HP)

                def advance_state(out, state, add, ar, ais, n):
                    u1, u2 = t1[:, :, :, 0:n], t2[:, :, :, 0:n]
                    a = tab[:, ar, js].unsqueeze(1).unsqueeze(3).broadcast_to([P, 2, HP, n])
                    link.mark(tt(u1, state, a, ALU.mult))
                    for ri in range(2):
                        link.mark(tt(u2[:, ri], state[:, 1 - ri],
                                     tab[:, ais + ri, js].unsqueeze(2).broadcast_to([P, HP, n]), ALU.mult))
                    link.settle()
                    link(tt(u1, u1, u2, ALU.add))
                    return tt(out, u1, add, ALU.add)

                dve.wait_ge(S["f_copied"], (half + 1) * HP // 2)
                e0 = ssm_e0[:]
                link(advance_state(e0, fv[:, :, :, :, 0], fv[:, :, :, :, 1], PA + 6, A4S, NC16))
                for q in range(2, QL):
                    link(advance_state(e0, e0, fv[:, :, :, :, q], PA + 6, A4S, NC16))
                if half:
                    dve.wait_ge(S["y_mm"], HT)
                dve.wait_ge(S["st_copied"], 1)
                dve.wait_ge(S["cz_tr"], 4)
                link.mark(dve.memset(gv[:, :, :, 0, 0], 0.0))
                for ri in range(2):
                    link.mark(dve.tensor_copy(gv[:, ri, :, PRUNS:, 0], st_in[:, ri, :, js].rearrange("p b j -> p j b")))
                link(dve.tensor_copy(gv[:, :, :, 1, 0], e0[:, :, :, 0]))
                for k in range(1, PRUNS):
                    end = k == PRUNS - 1
                    link(advance_state(st_prompt[:, :, js].unsqueeze(3) if end else gv[:, :, :, k + 1:k + 2, 0],
                                       gv[:, :, :, k:k + 1, 0], e0[:, :, :, k:k + 1], A16, A16S, 1))
                link(advance_state(st_out[:, :, :, js].rearrange("p r b j -> p r j b"), gv[:, :, :, PRUNS:, 0],
                                   e0[:, :, :, PRUNS:], A16, A16S, NB))
                for q in range(QL - 1):
                    ins = advance_state(gv[:, :, :, :, q + 1], gv[:, :, :, :, q], fv[:, :, :, :, q], PA + 6, A4S, NC16)
                    if q < QL - 2:
                        link(ins)
                ins.then_inc(S["g_ready"], 1)
                dve.wait_ge(S["g_ready"], half + 1)

            root(2)
            dve.wait_ge(S["x_new"], 2 * DT)
            for m in range(DT):
                if m >= 2:
                    dve.wait_ge(S["u_ready"], m - 1)
                tt(scaled[:, m % 2, :], x[:, m, :], rstd[:], ALU.mult).then_inc(S["u_scaled"], 1)
            build_z(0)
            build_z(1)
            dve.wait_ge(S["u_ready"], DT)
            states(0)
            states(1)
            for m in range(DT):
                dve.wait_ge(S["x_hi_ready"], split_base["glu"] + m + 1)
                order = "p (n r) -> p r n"
                tt(x_lo[:, m, :].rearrange(order, r=QL), y_r[:, m], x_hi[:, m, :].rearrange(order, r=QL).bitcast(F32),
                   ALU.subtract).then_inc(S["x_lo_ready"], 1)
            steps(2, glu_step)
            root(3)
            advance(gains, gain_col(0, 3, 0), 1, "ffn2", SPLITS[1])
            root(4)
            steps(3, in_step(1))
            steps(4, out_step)
            root(5)
            advance(half_gains, gain_col(0, 5, 0), 2, "kv", SPLITS[2])
            root(6)
            steps(5, scaled_step(kvT))
            for m in range(DT):
                lo("ffn1b", SPLITS[3], m)
            for g in range(0, 2 * DT * TT // 4, 2):
                dve.wait_ge(S["kv_tr"], g + 1)
                dve.tensor_copy(kv_dst(g), psum[:, 5 + g % 3, :]).then_inc(S["kv_copied_v"], 1)

            def none():
                pass

            def kv_left():
                dve.wait_ge(S["stored"], 16 * 10)

            steps(6, in_step(2), (none, kv_left))
            steps(7, out_step)
            root(7)
            advance(half_gains, gain_col(1, 1, 0), 3, "q", SPLITS[4])
            root(8)
            steps(8, scaled_step(qT))

            def copy_q(b):
                for g in range(2):
                    rows = slice(g * HD, (g + 1) * HD)
                    ins = dve.tensor_copy(q_blk[rows, :, g, :], qT[rows, :, bass.ds(b * LS + SEQ, LS)])
                ins.then_inc(S["q_ready"], 1)

            def copy_kt(b, kb):
                dve.wait_ge(S["kt_tr"], b * 8 + (2 * kb + 1))
                dve.tensor_copy(kT[:, 0:4, kb * P:(kb + 1) * P],
                                psum[:, 4 + 2 * (kb % 2), :].rearrange("p (a c) -> p a c", c=P)).then_inc(S["kt_copied_v"], 1)

            def copy_o(b):
                dve.wait_ge(S["o_tr"], b + 1)
                for g in range(2):
                    rows = slice(g * HD, (g + 1) * HD)
                    src = psum[rows, 6, 0:2 * P].rearrange("p (m g i) -> p m g i", g=2, i=LS)[:, :, g, :]
                    ins = dve.tensor_copy(oT[rows, :, bass.ds(b * LS + SEQ, LS)], src)
                ins.then_inc(S["o_ready"], 1)

            def stream(b, more, first=False):
                for hh in range(2):
                    dve.wait_ge(S["scored"], b * 2 + (hh + 1))
                    sc = psum[:, 2 * hh:2 * hh + 2, :].rearrange("p a b -> p (a b)")[:, 0:KN]
                    stt(prob[:, hh, :], sc, SCALE, bias_s[:, hh, :], ALU.mult, ALU.add).then_inc(S["soft_made"], 1)
                    dve.wait_ge(S["soft_made"], b * 2 + (hh + 1))
                    dve.tensor_reduce(row_s[:, hh, 0:1], prob[:, hh, :], AX_X, ALU.max, negate=True).then_inc(S["soft_in"], 1)
                if more:
                    copy_q(b + 1)
                for hh in range(2):
                    if more:
                        copy_kt(b + 1, hh)
                    dve.wait_ge(S["exped"], b * 2 + (hh + 1))
                    dve.reciprocal(row_s[:, hh, 2:3], row_s[:, hh, 1:2]).then_inc(S["recip_made"], 1)
                    dve.wait_ge(S["recip_made"], b * 2 + (hh + 1))
                    ts(prob[:, hh, :], prob[:, hh, :], row_s[:, hh, 2:3], None, ALU.mult).then_inc(S["prob_ready"], 1)
                if more:
                    copy_kt(b + 1, 2)
                if not first:
                    copy_o(b - 1)
                for hh in range(2):
                    dve.wait_ge(S["p_tr"], b * 2 + (hh + 1))
                    dve.tensor_copy(probT[0:LS, hh, KC:KC + P], psum[0:LS, 2 * hh + 1, 2 * P:3 * P]).then_inc(S["pt4_copied"], 1)
                if more:
                    copy_kt(b + 1, 3)
                for hh in range(2):
                    dve.wait_ge(S["pv_done"], b * 2 + (hh + 1))
                    dve.tensor_copy(o_rows[:, hh, :], psum[:, 2 * hh + 1, P:2 * P]).then_inc(S["o_rows_made"], 1)

            link(dve.memset(q_blk[:], 0.0))
            copy_q(0)
            for kb in range(KB):
                copy_kt(0, kb)
            dve.wait_ge(S["bias_landed"], 16 * NH)
            for hh in range(2):
                link.mark(dve.tensor_copy(bias_s[:, hh, 0:384], bias_s[:, hh, 384:385].broadcast_to([P, 384])))
            link.settle()
            stream(0, True, True)
            with dve.Fori(1, NB - 1) as b:
                stream(b, True)
            stream(NB - 1, False)
            copy_o(NB - 1)

            def head_bias(j, hh):
                return bias_p[:, bass.ds(j * 2 + hh, 1), :].rearrange("p o k -> p (o k)")

            def mask(part):
                dve.wait_ge(p_landed[part], 32)
                for c in (1, 3):
                    ins = dve.memset(bias_p[0:HD, part * NH // 2:(part + 1) * NH // 2, c * P - HD:c * P], NEG)
                ins.then_inc(S["bias_masked"], 1)
                dve.wait_ge(S["bias_masked"], part + 1)

            def soft(j, s):
                for hh in range(2):
                    dve.wait_ge(S["pscored"], j * 2 + (hh + 1))
                    stt(prob_p[:, s, hh, :], psum[:, 2 * s + hh, 0:3 * P], SCALE, head_bias(j, hh), ALU.mult,
                        ALU.add).then_inc(S["psoft_made"], 1)
                    dve.wait_ge(S["psoft_made"], j * 2 + (hh + 1))
                    dve.tensor_reduce(row_p[:, s, hh, 0:1], prob_p[:, s, hh, 0:P], AX_X, ALU.max, negate=True)
                    dve.tensor_reduce(row_p[:, s, hh, 1:2], prob_p[:, s, hh, P:3 * P], AX_X, ALU.max, negate=True).then_inc(S["psoft"], 1)

            def pair(j, s, more):
                if more:
                    soft(j + 1, 1 - s)
                for hh in range(2):
                    dve.wait_ge(S["pexped"], j * 2 + (hh + 1))
                    dve.reciprocal(row_p[:, s, hh, 4:6], row_p[:, s, hh, 2:4]).then_inc(S["precip_made"], 1)
                    dve.wait_ge(S["precip_made"], j * 2 + (hh + 1))
                    ts(prob_p[:, s, hh, 0:P], prob_p[:, s, hh, 0:P], row_p[:, s, hh, 4:5], None, ALU.mult)
                    ts(prob_p[:, s, hh, P:3 * P], prob_p[:, s, hh, P:3 * P], row_p[:, s, hh, 5:6], None, ALU.mult).then_inc(S["pprob"], 1)

            mask(0)
            soft(0, 0)
            for s in range(2):
                pair(s, s, True)
            mask(1)
            with dve.Fori(1, DT // 2 - 1) as turn:
                for s in range(2):
                    pair(turn * 2 + s, s, True)
            pair(DT - 2, 0, True)
            pair(DT - 1, 1, False)
            for m in range(DT):
                dve.wait_ge(S["x_hi_ready"], split_base["o"] + m + 1)
                tt(x_lo[:, m, :], oT[:, m, :], x_hi[:, m, :].bitcast(F32), ALU.subtract).then_inc(S["x_lo_ready"], 1)
            steps(9, o_step)
            root(9)
            advance(gains, gain_col(1, 3, 0), 4, "ffn2b", SPLITS[5])
            root(10)
            steps(10, in_step(3))
            steps(11, out_step)
            root(11)
            advance(half_gains, gain_col(1, 5, 0), 5)
            for g in range(0, 2 * TT, 2):
                dve.wait_ge(S["out_tr"], g + 1)
                dve.tensor_copy(out_dst(g), psum[:, 5 + g % 3, :]).then_inc(S["out_copied_v"], 1)

        @block.gpsimd
        def _(pool):
            pool.memset(ones[:], 1.0).then_inc(S["const_made"], 1)
            pool.memset(consts[:, 0:1], EPS).then_inc(S["const_made"], 1)
            pool.memset(consts[:, 1:2], math.pi / 2).then_inc(S["const_made"], 1)
            pool.memset(consts[:, 2:3], 0.0).then_inc(S["const_made"], 1)
            pool.wait_ge(S["const_made"], 4)

            def sums(j0, j1):
                def one(j):
                    if not isinstance(j, int) or j > 0:
                        pool.wait_ge(S["total_ready"], j * 1)
                    pool.wait_ge(S["squared"], j * DT + 1)
                    pool.tensor_tensor(ssum[:], sq[:, 0, :], consts[:, 2:3].broadcast_to([P, TOK]), ALU.add).then_inc(S["sq_added"], 1)
                    for m in range(1, DT):
                        pool.wait_ge(S["squared"], j * DT + (m + 1))
                        pool.wait_ge(S["sq_added"], j * DT + m)
                        pool.tensor_tensor(ssum[:], ssum[:], sq[:, m % 2, :], ALU.add).then_inc(S["sq_added"], 1)
                if j1 == j0 + 1:
                    one(j0)
                else:
                    with pool.Fori(j0, j1) as j:
                        one(j)

            sums(0, 1)
            sums(1, 3)
            link = Link(pool, S["pool_link"])
            a, b = (ca_tmp[:, i, :].rearrange("p (j c) -> p j c", j=HP) for i in range(2))
            pool.wait_ge(S["chunk_done"], STARTS[2])
            pool.memset(ssm_z2[:], 0.0).then_inc(S["z_zeroed"], 1)
            pool.wait_ge(S["cz_masked"], 4)
            pool.memset(ssm_m[:], 0.0).then_inc(S["m_zeroed"], 1)
            pool.wait_ge(S["total_ready"], 3)
            for half in range(2):
                js = slice(half * HP, (half + 1) * HP)
                pool.wait_ge(S["cz_ready"], 2 * half + 2)
                cr, cn = (c_z[:, half, ri, :].rearrange("p (j c) -> p j c", j=HP) for ri in range(2))
                pool.wait_ge(S["m_mm"], half + 1)
                for t in range(QL):
                    pr, pi = (tab[:, PA + 2 * t + ri, js].unsqueeze(2).broadcast_to([P, HP, 32]) for ri in range(2))
                    for ri, (u, v, op) in enumerate(((cr, cn, ALU.add), (cn, cr, ALU.subtract))):
                        link.mark(pool.tensor_tensor(a, u, pr, ALU.mult))
                        link(pool.tensor_tensor(b, v, pi, ALU.mult))
                        ins = pool.tensor_tensor(ca_of[half][:, ri, :, t, :], a, b, op)
                        if (t, ri) != (QL - 1, 1):
                            link(ins)
                ins.then_inc(S["ca_ready"], 1)
                pool.wait_ge(S["ca_ready"], half + 1)
            sums(3, NORMS)

        @block.tensor
        def _(pe):
            link = Link(pe, S["pe_link"])
            mm, tr = pe.matmul, pe.transpose

            def chunk(stage, s, n, parts=None, gate=None):
                kind = STAGES[stage][0]
                hi, lo = (h_hi, h_lo) if kind == "out" else (x_hi, x_lo)
                K = FT if kind == "out" else DT
                pe.wait_ge(S["w_lo_ready"], n + 1)
                if not isinstance(n, int) or n >= 2:
                    pe.wait_ge(S["acc_read"], n - 1)
                for k in range(K):
                    if gate is not None:
                        pe.wait_ge(gate[0], gate[1] + k)
                    for h in range(1 if kind == "out" else 2):
                        c = k * P if kind == "out" else k * 2 * P + h * P
                        out = acc(s, h)
                        mm(out, w_hi[s][:, c:c + P], hi[:, k, :], start=(k == 0), stop=False)
                        mm(out, w_hi[s][:, c:c + P], lo[:, k, :], start=False, stop=False)
                        ins = mm(out, w_lo[s][:, c:c + P], hi[:, k, :], start=False, stop=(k == K - 1))
                ins.then_inc(S["chunk_done"], 1)

            def products(stage, gate, after_first=None):
                n0, count = STARTS[stage], STAGES[stage][1]
                chunk(stage, 0, n0, gate=gate)
                if after_first is not None:
                    total(after_first)
                chunk(stage, 1, n0 + 1)
                with pe.Fori(1, count // 2) as turn:
                    i = turn * 2
                    for s in range(2):
                        chunk(stage, s, i + (n0 + s))

            def total(j):
                pe.wait_ge(S["sq_added"], DT * (j + 1))
                if j:
                    pe.wait_ge(S["std_ready"], j)
                mm(psum[:, TOT, 0:TOK], ones[:], ssum[:], start=True, stop=True).then_inc(S["total_ready"], 1)

            def x_gate(name):
                return S["x_lo_ready"], split_base[name] + 1

            pe.wait_ge(S["const_landed"], 16 * 4)
            tr(psum[:, 7, 0:104], gain_rows[:, :], ident[0:104, 0:104]).then_inc(S["gain_rows_t"], 1)
            pe.wait_ge(S["io_landed"], 32)
            yv = y[:].rearrange("p a b -> p (a b)").rearrange("p (t d) -> p t d", t=TT)
            for m in range(DT):
                if m >= 4:
                    pe.wait_ge(S["x_new"], m - 3)
                for t in range(TT):
                    ins = tr(psum[:, m % 4, t * P:(t + 1) * P], yv[:, t, m * P:(m + 1) * P], ident[:])
                ins.then_inc(S["x_transposed"], 1)
            pe.wait_ge(S["x_new"], DT)
            pe.wait_ge(S["const_made"], 3)
            products(0, x_gate("ffn1"), 0)
            products(1, (S["h_ready"], 1))
            pe.wait_ge(S["tables_t"], 1)
            for i in range(NTAB):
                ins = tr(psum[:, 5 + i // 16, (i % 16) * NPAIR:(i % 16 + 1) * NPAIR], prow[:, i, :], ident[0:NPAIR, 0:NPAIR])
            ins.then_inc(S["tab_tr"], 1)
            total(1)
            total(2)

            pe.wait_ge(S["ssm_landed"], 16 * 8)
            for i in range(4):
                ins = tr(psum[:, 7, i * P:(i + 1) * P], st_rows[:, i // 2, i % 2, :], ident[:])
            ins.then_inc(S["st_tr"], 1)
            stage = y[:].rearrange("p a b -> p (a b)")
            for half in range(2):
                for ri in range(2):
                    pe.wait_ge(S["cz_masked"], 2 * half + ri + 1)
                    if half:
                        pe.wait_ge(S["cz_ready"], ri + 1)
                    for t in range(HT):
                        c = ((2 * half + ri) * HT + t) * P
                        ins = tr(psum[:, 5 + ri, t * P:(t + 1) * P], stage[:, c:c + P], ident[:])
                    ins.then_inc(S["cz_tr"], 1)

            def transpose_z(half):
                pe.wait_ge(S["zn_ready"], half + 1)
                pe.wait_ge(S["cz_ready"], 4)
                for i in range(2 * HT):
                    n = half * 2 * HT + i
                    if n >= 3:
                        pe.wait_ge(S["z_copied"], n - 2)
                    for a in range(4):
                        z = z_of[half][:, i // HT, (i % HT) * 4 + a].rearrange("p s c -> p (s c)")
                        ins = tr(psum[:, 4 + n % 3, a * P:(a + 1) * P], z, ident[:])
                    ins.then_inc(S["z_tr"], 1)

            def matrices(half):
                pe.wait_ge(S["d_ready"], half + 1)
                if half:
                    pe.wait_ge(S["m_ready"], 1)
                else:
                    pe.wait_ge(S["st_copied"], 1)
                mm(psum[:, 7, :], ident[P - 32:P, :], d_diag[half][P - 32:P].rearrange("p j c -> p (j c)"), start=True, stop=False,
                   skip_group_check=True)
                for j in range(HP):
                    for ri in range(2):
                        ins = mm(psum[:, 7, j * 32:(j + 1) * 32], z_of[half][:, ri, j].rearrange("p s c -> p (s c)"),
                                 c_z[:, half, ri, j * 32:(j + 1) * 32], start=False, stop=(j == HP - 1 and ri == 1), skip_group_check=True)
                ins.then_inc(S["m_mm"], 1)

            def quads(half):
                pe.wait_ge(S["z_copied"], (half + 1) * 2 * HT)
                pe.wait_ge(S["u_landed"], 16 * 4 * QL)
                for i in range(HP // 2):
                    n = half * HP // 2 + i
                    if n >= 4:
                        pe.wait_ge(S["f_copied"], n - 3)
                    for a in range(2):
                        for ri in range(2):
                            c = (a * 2 + ri) * NQ
                            ins = mm(psum[:, n % 4, c:c + NQ], ssm_t[:, ri, 2 * i + a, :], u_q[:, half * HP + 2 * i + a, :], start=True, stop=True)
                    ins.then_inc(S["f_mm"], 1)

            def outputs(half):
                pe.wait_ge(S["m_ready"], half + 1)
                ca = ca_of[half]
                g = ssm_g[:].rearrange("p a b -> p (a b)").rearrange("p (r j n) -> p r j n", r=2, j=HP)
                for t in range(HT):
                    m = half * HT + t
                    if m >= 2:
                        pe.wait_ge(S["y_gelu"], m - 1)
                    bank = 5 + m % 2
                    for a in range(4):
                        mm(psum[:, bank, a * NQ:(a + 1) * NQ], ssm_m[:, 4 * t + a].rearrange("p s c -> p (s c)"), u_q[:, 4 * m + a, :],
                           start=(a == 0), stop=False, skip_group_check=True)
                    if t == 0:
                        pe.wait_ge(S["g_ready"], half + 1)
                        pe.wait_ge(S["ca_ready"], half + 1)
                    for a in range(4):
                        for ri in range(2):
                            ins = mm(psum[:, bank, a * NQ:(a + 1) * NQ], ca[:, ri, 4 * t + a].rearrange("p s c -> p (s c)"),
                                     g[:, ri, 4 * t + a, :], start=False, stop=(a == 3 and ri == 1), skip_group_check=True)
                    ins.then_inc(S["y_mm"], 1)

            transpose_z(0)
            quads(0)
            matrices(0)
            transpose_z(1)
            matrices(1)
            quads(1)
            outputs(0)
            outputs(1)
            for i in range(4):
                tr(psum[:, 7, i * P:(i + 1) * P], st_out[:].rearrange("p r b j -> p (r b j)")[:, i * P:(i + 1) * P], ident[:])
            for ri in range(2):
                ins = tr(psum[0:NPAIR, TOT, ri * P:(ri + 1) * P], st_prompt[:, ri, :], ident[:])
            ins.then_inc(S["st_tr2"], 1)
            pe.wait_ge(S["sout_ready"], 1)
            products(2, x_gate("glu"))
            total(3)
            products(3, x_gate("ffn2"), 4)
            products(4, (S["h_ready"], FT + 1))
            total(5)
            products(5, x_gate("kv"), 6)
            pe.wait_ge(S["acc_read"], STARTS[6])
            for g in range(2 * DT * TT // 4):
                if g >= 3:
                    pe.wait_ge(S["kv_copied_a" if (g - 3) % 2 else "kv_copied_v"], (g - 3) // 2 + 1)
                for a in range(4):
                    ins = tr(psum[:, 5 + g % 3, a * P:(a + 1) * P], kvT[:, (g % 4) * 4 + a, (g // 4) * P:(g // 4 + 1) * P], ident[:])
                ins.then_inc(S["kv_tr"], 1)
            products(6, x_gate("ffn1b"))
            products(7, (S["h_ready"], 2 * FT + 1))
            total(7)
            products(8, x_gate("q"), 8)

            def transpose_k(b, kb, first=False):
                for g in range(2):
                    if g == 0:
                        pe.wait_ge(k_landed[kb], b * 16 + 16)
                    if not first or kb >= 2:
                        pe.wait_ge(S["kt_copied_a" if g else "kt_copied_v"], b * KB + (kb - 1))
                    for a in range(4):
                        c = (g * 4 + a) * P
                        ins = tr(psum[:, 4 + 2 * (kb % 2) + g, a * P:(a + 1) * P], k_raw[:, kb, c:c + P], ident[:])
                    ins.then_inc(S["kt_tr"], 1)

            def transpose_o(b, more):
                pe.wait_ge(S["o_rows_made"], b * 2)
                if more:
                    pe.wait_ge(S["kt_copied_v"], b * KB + (KB + 2))
                for hh in range(2):
                    ins = tr(psum[:, 6, hh * P:(hh + 1) * P], o_rows[:, hh, :], ident[:])
                ins.then_inc(S["o_tr"], 1)

            def stream(b, more, first=False):
                for n in ("kt_copied_a", "kt_copied_v"):
                    pe.wait_ge(S[n], b * KB + KB)
                pe.wait_ge(S["kn_landed"], b * 16 + 16)
                pe.wait_ge(S["q_ready"], b + 1)
                for hh in range(2):
                    if not first:
                        pe.wait_ge(S["o_rows_made"], b * 2 + (hh - 1))
                    for a in range(4):
                        lhs = q_blk[:, 4 * hh + a].rearrange("p g i -> p (g i)")
                        rows = slice(32 * a, 32 * a + 32)
                        mm(psum[rows, 2 * hh, :], lhs, kT[:, 4 * hh + a, 0:KC], start=True, stop=True)
                        ins = mm(psum[rows, 2 * hh + 1, 0:LS], lhs, kT[:, 4 * hh + a, KC:KN], start=True, stop=True)
                    ins.then_inc(S["scored"], 1)
                if more:
                    for kb in range(KB - 1):
                        transpose_k(b + 1, kb)
                if not first:
                    transpose_o(b, more)
                for hh in range(2):
                    pe.wait_ge(S["prob_ready"], b * 2 + (hh + 1))
                    for kb in range(KB):
                        tr(psum[:, 2 * hh, kb * P:(kb + 1) * P], prob[:, hh, kb * P:(kb + 1) * P], ident[:])
                    tr(psum[0:LS, 2 * hh + 1, 2 * P:3 * P], prob[:, hh, KC:KN], ident[:]).then_inc(S["p_tr"], 1)
                if more:
                    if not first:
                        pe.wait_ge(S["o_ready"], b)
                    transpose_k(b + 1, KB - 1)
                for hh in range(2):
                    pe.wait_ge(S["pt_copied"], b * 2 + (hh + 1))
                    pe.wait_ge(S["pt4_copied"], b * 2 + (hh + 1))
                    pe.wait_ge(v_landed[hh], b * 32 + 32)
                    for kb in range(KB + 1):
                        n = P if kb < KB else LS
                        for a in range(4):
                            c, rows = (4 * hh + a) * P, slice(32 * a, 32 * a + 32)
                            ins = mm(psum[rows, 2 * hh + 1, P:2 * P], probT[0:n, hh, kb * P + 32 * a:kb * P + 32 * a + 32],
                                     v_raw[0:n, kb, c:c + P], start=(kb == 0), stop=(kb == KB))
                    ins.then_inc(S["pv_done"], 1)

            pe.wait_ge(S["acc_read"], STARTS[9])
            for kb in range(KB):
                transpose_k(0, kb, True)
            stream(0, True, True)
            with pe.Fori(1, NB - 1) as b:
                stream(b, True)
            stream(NB - 1, False)
            pe.wait_ge(S["o_ready"], NB - 1)
            transpose_o(NB, False)

            def score(j, s):
                pe.wait_ge(S["qp_ready"], j + 1)
                for hh in range(2):
                    rows = slice(hh * HD, (hh + 1) * HD)
                    bank = 2 * s + hh
                    mm(psum[:, bank, 0:P], q_p[rows, s, 0:P], kTp[rows, s, 0:P], start=True, stop=True)
                    mm(psum[:, bank, P:3 * P], q_p[rows, s, P:2 * P], kTp[rows, s, :], start=True, stop=True).then_inc(S["pscored"], 1)

            def pair(j, s, more, first=False):
                for hh in range(2):
                    pe.wait_ge(S["pprob"], j * 2 + (hh + 1))
                    for a in range(3):
                        ins = tr(psum[:, 4 + hh, a * P:(a + 1) * P], prob_p[:, s, hh, a * P:(a + 1) * P], ident[:])
                    ins.then_inc(S["pp_tr"], 1)
                if more:
                    score(j + 2, s)
                pe.wait_ge(S["vp_ready"], j + 1)
                for hh in range(2):
                    rows = slice(hh * HD, (hh + 1) * HD)
                    if not first:
                        pe.wait_ge(S["po_ready"], j * 2 + (hh - 1))
                    pe.wait_ge(S["ppt_copied"], j * 2 + (hh + 1))
                    mm(psum[rows, 6 + hh, 0:P], v_p[:, s, 0, rows], probT_p[:, hh, 0:P], start=True, stop=True)
                    mm(psum[rows, 6 + hh, P:2 * P], v_p[:, s, 0, rows], probT_p[:, hh, P:2 * P], start=True, stop=False)
                    mm(psum[rows, 6 + hh, P:2 * P], v_p[:, s, 1, rows], probT_p[:, hh, 2 * P:3 * P], start=False,
                       stop=True).then_inc(S["ppv"], 1)

            pe.wait_ge(S["kvp_landed"], 32)
            pe.wait_ge(S["o_ready"], NB)
            for s in range(2):
                score(s, s)
            for s in range(2):
                pair(s, s, True, s == 0)
            with pe.Fori(1, DT // 2 - 1) as turn:
                for s in range(2):
                    pair(turn * 2 + s, s, True)
            pair(DT - 2, 0, False)
            pair(DT - 1, 1, False)
            products(9, x_gate("o"))
            total(9)
            products(10, x_gate("ffn2b"), 10)
            products(11, (S["h_ready"], 3 * FT + 1))
            total(11)
            for g in range(2 * TT):
                if g < 2:
                    pe.wait_ge(S["x_new"], 6 * DT + 4 * (g + 1))
                if g >= 3:
                    pe.wait_ge(S["out_copied_a" if (g - 3) % 2 else "out_copied_v"], (g - 3) // 2 + 1)
                for a in range(4):
                    m = (g % 2) * 4 + a
                    ins = tr(psum[:, 5 + g % 3, a * P:(a + 1) * P], x[:, m, (g // 2) * P:(g // 2 + 1) * P], ident[:])
                ins.then_inc(S["out_tr"], 1)


_OUTS = [("y_prompt", (1, SEQ, D)), ("y_sample", (NB, LS, D)), ("ssm_re_p", (1, 1, NG, NS)), ("ssm_im_p", (1, 1, NG, NS)),
         ("k_p", (1, SEQ, NH, HD)), ("v_p", (1, SEQ, NH, HD)), ("ssm_re_s", (1, NB, NG, NS)), ("ssm_im_s", (1, NB, NG, NS)),
         ("k_s", (NB, LS, NH, HD)), ("v_s", (NB, LS, NH, HD))]


def kernel(**inputs):
    import numpy as _np
    import concourse.bacc as _bacc
    from concourse.bass_utils import run_bass_kernel_spmd as _run

    nc = _bacc.Bacc("TRN2", target_bir_lowering=False, num_devices=1)
    arrays = {n: _np.ascontiguousarray(a) for n, a in inputs.items() if n != "attn_rel_bias"}
    arrays["bias_reversed"] = _np.ascontiguousarray(_np.asarray(inputs["attn_rel_bias"])[0, :, ::-1])
    i = _np.arange(P)
    arrays["c_ident"] = _np.eye(P, dtype=_np.float32)
    arrays["c_parmask"] = (i[:, None] // SC % 2 == _np.arange(2)[None, :]).astype(_np.float32)
    A = inputs_of(nc, {n: a.shape for n, a in arrays.items()})
    O = {n: nc.dram_tensor(f"out_{n}_dram", s, F32, kind="ExternalOutput").ap() for n, s in _OUTS}
    scratch = {"bias": nc.dram_tensor("scratch_bias", [NH, PAD + NREL], F32).ap(),
               "tiles": nc.dram_tensor("scratch_tiles", [NH, P, SEQ], F32).ap(),
               "kT": nc.dram_tensor("scratch_kT", [P, DT * TOK], F32).ap(),
               "v": nc.dram_tensor("scratch_v", [TOK, D], F32).ap()}
    build(nc, A, O, scratch)
    r = _run(nc, [{f"in_{n}_dram": a for n, a in arrays.items()}], core_ids=[0])
    return tuple(r.results[0][f"out_{n}_dram"] for n, _ in _OUTS)
```
